# Optimizing a Trainium2 kernel written in Bass

```python
import math
import jax, jax.numpy as jnp
from jax import lax
import numpy as np

D_MODEL = 2048
BATCH = 1
SEQ = 256
DEPTH = 2

N_DIFF_HEADS = 8
DIFF_HEAD_DIM = 64
DIFF_V_DIM = 2 * DIFF_HEAD_DIM
ATTN_WIDTH = N_DIFF_HEADS * DIFF_V_DIM
CONV_WIDTH = D_MODEL - ATTN_WIDTH
CONV_K = 3
IN_PROJ_WIDTH = 3 * ATTN_WIDTH + 3 * CONV_WIDTH
D_FF = -(-8 * D_MODEL // (3 * 256)) * 256
ROPE_THETA = 10000.0
EPS = 1e-6
Q_BLOCK = 128

kernel_name = 'hybrid_diffattn_shortconv_encoder'

def rmsnorm(t, g):
    tf = t.astype(jnp.float32)
    tf = tf * lax.rsqrt(jnp.mean(tf * tf, axis=-1, keepdims=True) + EPS)
    return (tf * g.astype(jnp.float32)).astype(t.dtype)

def rope_tables(seq):
    pos = jnp.arange(seq, dtype=jnp.float32)
    inv_freq = ROPE_THETA ** (-jnp.arange(0, DIFF_HEAD_DIM, 2, dtype=jnp.float32) / DIFF_HEAD_DIM)
    ang = pos[:, None] * inv_freq[None, :]
    return jnp.cos(ang)[:, None, :], jnp.sin(ang)[:, None, :]

def apply_rope(t, cos, sin):
    tf = t.astype(jnp.float32)
    t1, t2 = jnp.split(tf, 2, axis=-1)
    return jnp.concatenate([t1 * cos - t2 * sin, t2 * cos + t1 * sin], axis=-1).astype(t.dtype)

def diff_attention(q, k, v, lam):
    b, s = q.shape[0], q.shape[1]
    nb = s // Q_BLOCK
    scale = DIFF_HEAD_DIM ** -0.5
    qf = (q.astype(jnp.float32) * scale).reshape(b, nb, Q_BLOCK, 2 * N_DIFF_HEADS, DIFF_HEAD_DIM)
    qf = qf.transpose(1, 0, 2, 3, 4)
    kf = k.astype(jnp.float32)

    def one_block(qb):
        sc = jnp.einsum('bqhd,bkhd->bhqk', qb, kf)
        p = jax.nn.softmax(sc, axis=-1).reshape(b, N_DIFF_HEADS, 2, Q_BLOCK, s)
        w = p[:, :, 0] - lam * p[:, :, 1]
        return jnp.einsum('bhqk,bkhe->bqhe', w.astype(v.dtype), v)

    o = lax.map(one_block, qf)
    return o.transpose(1, 0, 2, 3, 4).reshape(b, s, N_DIFF_HEADS, DIFF_V_DIM)

def short_gated_conv(gate_b, gate_c, u, w):
    z = gate_c * u
    zp = jnp.pad(z, ((0, 0), (1, 1), (0, 0)))
    y = zp[:, :-2] * w[0] + zp[:, 1:-1] * w[1] + zp[:, 2:] * w[2]
    return gate_b * y

def setup_inputs(seed: int = 0) -> dict:
    key = jax.random.key(seed)
    ks = jax.random.split(key, 15)
    f32 = jnp.float32
    nrm = lambda k, shape, s: jax.random.normal(k, shape, f32) * s
    return {
        'x': nrm(ks[0], (BATCH, SEQ, D_MODEL), 1.0),
        'norm_mix': 1.0 + nrm(ks[1], (DEPTH, D_MODEL), 0.02),
        'w_in': nrm(ks[2], (DEPTH, D_MODEL, IN_PROJ_WIDTH), D_MODEL ** -0.5),
        'lambda_q1': nrm(ks[3], (DEPTH, DIFF_HEAD_DIM), 0.1),
        'lambda_k1': nrm(ks[4], (DEPTH, DIFF_HEAD_DIM), 0.1),
        'lambda_q2': nrm(ks[5], (DEPTH, DIFF_HEAD_DIM), 0.1),
        'lambda_k2': nrm(ks[6], (DEPTH, DIFF_HEAD_DIM), 0.1),
        'subln': 1.0 + nrm(ks[7], (DEPTH, DIFF_V_DIM), 0.02),
        'conv_w': nrm(ks[8], (DEPTH, CONV_K, CONV_WIDTH), CONV_K ** -0.5),
        'w_out': nrm(ks[9], (DEPTH, D_MODEL, D_MODEL), D_MODEL ** -0.5),
        'norm_ffn': 1.0 + nrm(ks[10], (DEPTH, D_MODEL), 0.02),
        'w_gate': nrm(ks[11], (DEPTH, D_MODEL, D_FF), D_MODEL ** -0.5),
        'w_up': nrm(ks[12], (DEPTH, D_MODEL, D_FF), D_MODEL ** -0.5),
        'w_down': nrm(ks[13], (DEPTH, D_FF, D_MODEL), D_FF ** -0.5),
        'norm_final': 1.0 + nrm(ks[14], (D_MODEL,), 0.02),
    }

def reference(x, norm_mix, w_in, lambda_q1, lambda_k1, lambda_q2, lambda_k2, subln,
              conv_w, w_out, norm_ffn, w_gate, w_up, w_down, norm_final):
    b, s, _ = x.shape
    cos, sin = rope_tables(s)
    splits = [ATTN_WIDTH, 2 * ATTN_WIDTH, 3 * ATTN_WIDTH,
              3 * ATTN_WIDTH + CONV_WIDTH, 3 * ATTN_WIDTH + 2 * CONV_WIDTH]
    for l in range(DEPTH):
        lam_init = 0.8 - 0.6 * math.exp(-0.3 * l)
        h = rmsnorm(x, norm_mix[l])
        proj = h @ w_in[l]
        q, k, v, gate_b, gate_c, u = jnp.split(proj, splits, axis=-1)
        q = apply_rope(q.reshape(b, s, 2 * N_DIFF_HEADS, DIFF_HEAD_DIM), cos, sin)
        k = apply_rope(k.reshape(b, s, 2 * N_DIFF_HEADS, DIFF_HEAD_DIM), cos, sin)
        v = v.reshape(b, s, N_DIFF_HEADS, DIFF_V_DIM)
        lam = (jnp.exp(jnp.sum(lambda_q1[l].astype(jnp.float32) * lambda_k1[l].astype(jnp.float32)))
               - jnp.exp(jnp.sum(lambda_q2[l].astype(jnp.float32) * lambda_k2[l].astype(jnp.float32)))
               + lam_init)
        o_attn = diff_attention(q, k, v, lam)
        o_attn = (rmsnorm(o_attn, subln[l]) * (1.0 - lam_init)).reshape(b, s, ATTN_WIDTH)
        o_conv = short_gated_conv(gate_b, gate_c, u, conv_w[l])
        x = x + jnp.concatenate([o_attn.astype(x.dtype), o_conv.astype(x.dtype)], axis=-1) @ w_out[l]
        h = rmsnorm(x, norm_ffn[l])
        x = x + (jax.nn.silu(h @ w_gate[l]) * (h @ w_up[l])) @ w_down[l]
    return rmsnorm(x, norm_final)


_drawn_inputs = setup_inputs


def setup_inputs(seed=0):
    import zlib

    import numpy as np

    out = dict(_drawn_inputs(seed))
    spreads = {}
    factors = {'subln': 4.078, 'norm_ffn': 3.237, 'norm_final': 2.782}
    for name, (base, spread) in spreads.items():
        noise = np.random.default_rng([zlib.crc32(name.encode()), seed]).standard_normal(out[name].shape)
        drawn = base * np.exp(spread * noise) if base else spread * noise
        out[name] = __import__('jax').numpy.asarray(drawn.astype(out[name].dtype))
    for name, factor in factors.items():
        out[name] = (out[name] * factor).astype(out[name].dtype)
    return out
```

```python
import math

import numpy as np
from concourse import mybir
import concourse.bass as bass

F32 = mybir.dt.float32
F32R = mybir.dt.float32r
ALU = mybir.AluOpType
ACT = mybir.ActivationFunctionType
AX_X = mybir.AxisListType.X

P = 128
S = 256
QT = S // P
DM = 2048
DEPTH = 2
HEADS = 8
HD = 64
AW = HEADS * 2 * HD
CW = DM - AW
FF = -(-8 * DM // (3 * 256)) * 256
EPS = 1e-6
THETA = 10000.0
KT = DM // P
FT = FF // P
CT = CW // P
COLS = 512
BT = COLS // P
UNIT_KT = 2
LOAD_KT = 2 * UNIT_KT
NRAW = 4
NSPLIT = 4

NQK = 2 * AW // COLS
NV = AW // COLS
NG = CW // COLS
NOUT = DM // COLS
NGU = 2 * FF // COLS
NDOWN = DM // COLS
V0 = NQK
B0 = V0 + NV
C0 = B0 + NG
U0 = C0 + NG
OUT0 = U0 + NG
GU0 = OUT0 + NOUT
DOWN0 = GU0 + NGU
UNITS = KT // UNIT_KT
DUNITS = FT // UNIT_KT
LOADS = UNITS // 2
DLOADS = DUNITS // 2
UNITS_LAYER = DOWN0 * UNITS + NDOWN * DUNITS
TILES_LAYER = BT * (DOWN0 + NDOWN) - NV * (BT - QT)
RELEASES_LAYER = DOWN0 * (UNITS - 2) + NDOWN * (DUNITS - 2)
LOW_LAYER = BT * (DOWN0 + NDOWN - NV)
PRE = KT
SPLIT_BIAS = 2 * NRAW
RELEASE_BIAS = 2
PAIR_USES = [len(range(s, 2 * DLOADS, NRAW)) for s in range(NRAW)]
LAYER_USES = [DOWN0 + NDOWN // 2 * PAIR_USES[s] for s in range(NRAW)]
OUT_ORDER = [0, 1, 2, 3, 4, 5, 8, 9, 10, 11, 12, 13, 14, 15, 6, 7]
GU_COLS = [0, 2, 1, 3]
PLAIN = [0, 1, 2, 3]

C_MIX = 0
C_FIN = C_MIX + DEPTH * KT
C_FFN = C_FIN + KT
C_CONV = C_FFN + DEPTH * KT
C_SUB = C_CONV + DEPTH * 3 * CT
N_CONST = C_SUB + DEPTH


class Place:

    def __init__(self, layer, b, down=None):
        self.down = down
        self.layer = layer
        if down is None:
            self.units = UNITS
            early = isinstance(b, int) and b < B0
            tiles = (BT * b if b <= V0 else BT * V0 + QT * (b - V0)) if early else BT * b - NV * (BT - QT)
            self.unit0 = layer * UNITS_LAYER + b * UNITS
            self.released = layer * RELEASES_LAYER + (b * (UNITS - 2) + RELEASE_BIAS)
            low = b if early else b - NV
            self.slot0 = 0
            self.load0 = 0
            self.b = b
        else:
            self.units = DUNITS
            tiles = BT * (DOWN0 + down) - NV * (BT - QT)
            self.unit0 = layer * UNITS_LAYER + (down * DUNITS + DOWN0 * UNITS)
            self.released = layer * RELEASES_LAYER + (down * (DUNITS - 2) + DOWN0 * (UNITS - 2) + RELEASE_BIAS)
            low = DOWN0 + down - NV
            self.slot0 = down % 2 * DUNITS % NSPLIT
            self.load0 = down % 2 * DLOADS
        self.tile0 = layer * TILES_LAYER + (PRE + tiles)
        self.low0 = layer * LOW_LAYER + BT * low

    def slot(self, k):
        return (self.slot0 + k) % NSPLIT

    def raw_slot(self, k):
        return (self.load0 + k // 2) % NRAW

    def landed(self, k):
        s = self.raw_slot(k)
        if self.down is None:
            return self.layer * (32 * LAYER_USES[s]) + (self.b * 32 + 32)
        n = DOWN0 + self.down // 2 * PAIR_USES[s] + (self.load0 + k // 2) // NRAW
        return self.layer * (32 * LAYER_USES[s]) + 32 * (n + 1)


class EarlyPlace(Place):

    def __init__(self, layer, b):
        Place.__init__(self, layer, b)
        self.tile0 = layer * TILES_LAYER + (b * BT + PRE)
        self.low0 = layer * LOW_LAYER + b * BT


def build_program(nc, x, w_in, w_out, w_gate, w_up, w_down, consts_d, lambdas_d, tables_d, ident_d, out):
    start = -(-nc.sbuf_base // 32) * 32
    end = nc.sbuf_top
    place = [start]

    def at(name, shape, dtype, offset):
        return nc.alloc_sbuf_tensor_at(name, shape, dtype, offset=offset)

    def put(name, shape, dtype):
        offset = place[0]
        place[0] = offset + -(-int(np.prod(shape[1:])) * 4 // 32) * 32
        assert place[0] <= end, (name, place[0], end)
        return at(name, shape, dtype, offset)

    raw = put("raw", [P, NRAW, LOAD_KT, COLS], F32)
    whi = put("whi", [P, NSPLIT, UNIT_KT, COLS], F32R)
    wlo = put("wlo", [P, NSPLIT, UNIT_KT, COLS], F32R)
    resid = put("resid", [P, KT, S], F32)
    xg = put("xg", [P, KT, 2 * S], F32R)
    shared = place[0]
    hidden = put("hidden", [P, FT, 2 * S], F32R)
    shared_end = place[0]
    ev = put("ev", [P, BT, S], F32)
    sqacc = put("sqacc", [P, S], F32)
    rms_bc = put("rms_bc", [P, S], F32)
    consts = put("consts", [P, N_CONST], F32)
    ident = put("ident", [P, P], F32)
    ones = put("ones", [P, 1], F32)
    neg_half = put("neg_half", [P, QT], F32)
    inv_width = put("inv_width", [P, QT], F32)
    eps = put("eps", [P, QT], F32)
    q_scale = put("q_scale", [P, 1], F32)
    mean_sq = put("mean_sq", [P, QT], F32)
    rms_tok = put("rms_tok", [P, QT], F32)
    neg_lam = put("neg_lam", [P, DEPTH], F32)
    sub_gain = put("sub_gain", [P, DEPTH], F32)
    neg_max = put("neg_max", [P, 2 * QT], F32)
    exp_sum = put("exp_sum", [P, 2 * QT], F32)
    exp_inv = put("exp_inv", [P, 2 * QT], F32)
    o_sq = put("o_sq", [P, QT], F32)
    o_ms = put("o_ms", [P, QT], F32)
    o_rms = put("o_rms", [P, QT], F32)

    spot = [shared]

    def share(name, shape, dtype):
        offset = spot[0]
        spot[0] = offset + int(np.prod(shape[1:])) * 4
        assert spot[0] <= shared_end, name
        return at(name, shape, dtype, offset)

    qk = share("qk", [P, 2 * HEADS, S], F32)
    gates = share("gates", [P, 2 * CT, S], F32)
    v_tok = share("v_tok", [P, QT, AW], F32)
    mixed = share("mixed", [P, KT, 2 * S], F32R)
    swapped = share("swapped", [P, BT, S], F32)
    cos_r = share("cos_r", [P, S], F32)
    sin_r = share("sin_r", [P, S], F32)
    rms2_bc = share("rms2_bc", [P, S], F32)
    q_head = share("q_head", [P, S], F32)
    k_head = share("k_head", [P, S], F32)
    probs = share("probs", [P, 2, QT, S], F32)
    wt = share("wt", [P, QT, S], F32)
    o_tok = share("o_tok", [P, QT, P], F32)
    x_tok = at("x_tok", [P, QT, DM], F32, shared)
    lambdas = at("lambdas", [P, DEPTH, 2, 2, HD], F32, shared + 4 * QT * DM)
    lam_prod = at("lam_prod", [P, DEPTH * 2, HD], F32, shared + 4 * (QT * DM + DEPTH * 4 * HD))
    lam_sum = at("lam_sum", [P, DEPTH * 2], F32, shared + 4 * (QT * DM + DEPTH * 6 * HD))
    lam_exp = at("lam_exp", [P, DEPTH * 2], F32, shared + 4 * (QT * DM + DEPTH * 6 * HD + 16))
    lam_dif = at("lam_dif", [P, DEPTH], F32, shared + 4 * (QT * DM + DEPTH * 6 * HD + 32))

    bank = [nc.alloc_psum_tensor(f"bank{i}", [P, COLS], F32) for i in range(8)]
    SCORE = [bank[4], bank[5]]
    TURN = bank[6]
    MIX = bank[7]

    sem = nc.alloc_semaphore
    raw_landed = [sem(f"raw_landed{i}") for i in range(NRAW)]
    x_landed = sem("x_landed")
    small_landed = sem("small_landed")
    tables_landed = sem("tables_landed")
    swap_landed = sem("swap_landed")
    stored = sem("stored")
    tile_done = sem("tile_done")
    unit_released = sem("unit_released")
    squares_summed = sem("squares_summed")
    rms_spread = sem("rms_spread")
    scores_done = sem("scores_done")
    turned = sem("turned")
    heads_mixed = sem("heads_mixed")
    heads_turned = sem("heads_turned")
    hi_ready = sem("hi_ready")
    low_copied = sem("low_copied")
    xg_hi = sem("xg_hi")
    squared = sem("squared")
    lam_exped = sem("lam_exped")
    silu_done = sem("silu_done")
    hidden_hi = sem("hidden_hi")
    conv_mid = sem("conv_mid")
    conv_hi = sem("conv_hi")
    probs_done = sem("probs_done")
    wt_copied = sem("wt_copied")
    o_squared = sem("o_squared")
    o_hi = sem("o_hi")
    weights_ready = sem("weights_ready")
    bank_free = sem("bank_free")
    set_up = sem("set_up")
    lam_step = sem("lam_step")
    x_updated = sem("x_updated")
    xg_ready = sem("xg_ready")
    sq_added = sem("sq_added")
    ms_ready = sem("ms_ready")
    rms_copied = sem("rms_copied")
    tables_ready = sem("tables_ready")
    rope_step = sem("rope_step")
    rope_done = sem("rope_done")
    gate_stored = sem("gate_stored")
    z_ready = sem("z_ready")
    conv_step = sem("conv_step")
    conv_ready = sem("conv_ready")
    max_ready = sem("max_ready")
    w_step = sem("w_step")
    o_scaled = sem("o_scaled")
    o_ready = sem("o_ready")
    gate_scaled = sem("gate_scaled")
    up_scaled = sem("up_scaled")
    hidden_f32 = sem("hidden_f32")
    hidden_ready = sem("hidden_ready")
    out_scaled = sem("out_scaled")
    out_ready = sem("out_ready")
    rms_ready = sem("rms_ready")
    staged = sem("staged")
    o_ms_ready = sem("o_ms_ready")
    o_rms_ready = sem("o_rms_ready")
    gated = sem("gated")

    ds = bass.ds
    lo_bits = lambda ap: ap.bitcast(F32)

    def over_tiles(ap):
        return ap.unsqueeze(1).to_broadcast([P, BT, S])

    w_in_v = w_in.rearrange("l (t p) n -> p l t n", p=P)
    w_out_v = w_out.rearrange("l (t p) n -> p l t n", p=P)
    w_gate_v = w_gate.rearrange("l (t p) n -> p l t n", p=P)
    w_up_v = w_up.rearrange("l (t p) n -> p l t n", p=P)
    w_down_v = w_down.rearrange("l (t p) n -> p l t n", p=P)

    def constants_set(eng):
        eng.wait_ge(set_up, 4)

    with nc.Block() as block:

        @block.sync
        def _(sp):
            sp.dma_start(x_tok[:], x.rearrange("o (q p) n -> p (o q) n", p=P)).then_inc(x_landed, 16)

            def slot_free(load, prior):
                sp.wait_ge(weights_ready, load * 2 + (SPLIT_BIAS + 2 - 2 * prior))

            def rows(slot, half):
                return raw[:, slot, UNIT_KT * half:UNIT_KT * (half + 1), :].unsqueeze(1)

            def load(src, layer, number, slot, kts, col, prior=NRAW):
                slot_free(number, prior)
                for half in range(2):
                    t = kts[UNIT_KT * half]
                    sp.dma_start(rows(slot, half), src[:, ds(layer, 1), t:t + UNIT_KT, ds(col, COLS)]
                                 ).then_inc(raw_landed[slot], 16)

            def plain_block(src, layer, b, col, order=tuple(range(KT)), priors=(NRAW,) * NRAW):
                for j in range(LOADS):
                    load(src, layer, layer * (UNITS_LAYER // 2) + (b * LOADS + j), j,
                         order[LOAD_KT * j:LOAD_KT * (j + 1)], col, priors[j])

            with sp.Fori(0, DEPTH) as layer:
                plain_block(w_in_v, layer, 0, 0, priors=(2, 2, 4, 4))
                with sp.Fori(1, OUT0) as b:
                    plain_block(w_in_v, layer, b, b * COLS)
                with sp.Fori(OUT0, GU0) as b:
                    plain_block(w_out_v, layer, b, b * COLS - OUT0 * COLS, order=OUT_ORDER)
                with sp.Fori(GU0, DOWN0) as b:
                    for j in range(LOADS):
                        slot_free(layer * (UNITS_LAYER // 2) + (b * LOADS + j), NRAW)
                        for half, src in ((0, w_gate_v), (1, w_up_v)):
                            sp.dma_start(raw[:, j, :, half * S:(half + 1) * S].unsqueeze(1),
                                         src[:, ds(layer, 1), LOAD_KT * j:LOAD_KT * (j + 1),
                                             ds(b * S - GU0 * S, S)]).then_inc(raw_landed[j], 16)
                with sp.Fori(0, NDOWN // 2) as pair:
                    for j in range(2 * DLOADS):
                        k = LOAD_KT * (j % DLOADS)
                        load(w_down_v, layer,
                             layer * (UNITS_LAYER // 2) + (pair * (2 * DLOADS) + DOWN0 * LOADS + j),
                             j % NRAW, range(k, k + LOAD_KT),
                             pair * (2 * COLS) + j // DLOADS * COLS, 2 if j < 2 else NRAW)
            for g in range(QT * BT):
                q, c = divmod(g, BT)
                sp.wait_ge(out_ready, g + 1)
                sp.dma_start(out[0, P * q:P * (q + 1), COLS * c:COLS * (c + 1)],
                             x_tok[:, q, COLS * c:COLS * (c + 1)]).then_inc(stored, 16)
            sp.wait_ge(stored, 16 * QT * BT)

        @block.gpsimd
        def _(pool):
            pool.dma_start(ident[:], ident_d).then_inc(small_landed, 16)
            pool.dma_start(consts[:], consts_d).then_inc(small_landed, 16)
            pool.dma_start(lambdas[:], lambdas_d).then_inc(small_landed, 16)

            def rms(norm):
                pool.wait_ge(ms_ready, norm + 1)
                pool.tensor_tensor(rms_tok[:], mean_sq[:], neg_half[:], ALU.pow).then_inc(rms_ready, 1)

            def swap(layer, c):
                pool.wait_ge(bank_free, layer * TILES_LAYER + (c * BT + PRE + BT))
                for r in range(4):
                    pool.dma_start(swapped[32 * r:32 * r + 32],
                                   qk[32 * (r ^ 1):32 * (r ^ 1) + 32, ds(c * BT, BT), :]).then_inc(swap_landed, 16)

            def stage(layer, h):
                constants_set(pool)
                pool.tensor_tensor(q_head[:].unsqueeze(1), qk[:, ds(h, 1), :],
                                   q_scale[:].unsqueeze(1).to_broadcast([P, 1, S]), ALU.mult)
                pool.tensor_copy(k_head[:].unsqueeze(1), qk[:, ds(h + HEADS, 1), :]).then_inc(staged, 1)

            def head_rms(layer, h):
                pool.wait_ge(o_squared, layer * HEADS + (h + 1))
                pool.tensor_tensor(o_ms[:], o_sq[:], inv_width[:], ALU.mult).then_inc(o_ms_ready, 1)
                pool.wait_ge(o_ms_ready, layer * (2 * HEADS) + (h * 2 + 1))
                pool.tensor_tensor(o_ms[:], o_ms[:], eps[:], ALU.add).then_inc(o_ms_ready, 1)
                pool.wait_ge(o_ms_ready, layer * (2 * HEADS) + (h * 2 + 2))
                pool.tensor_tensor(o_rms[:], o_ms[:], neg_half[:], ALU.pow).then_inc(o_rms_ready, 1)

            def gate(layer, u):
                for j in range(BT):
                    pool.wait_ge(conv_step, layer * (2 * CT) + (2 * BT * u + BT + j + 1))
                    pool.tensor_tensor(ev[:, j, :], ev[:, j, :], gates[:, BT * u + j, :], ALU.mult).then_inc(gated, 1)

            with pool.Fori(0, DEPTH) as layer:
                rms(layer * 2)
                with pool.Fori(0, NQK) as c:
                    pool.wait_ge(rope_done, layer * NQK + (c + 1))
                    swap(layer, c)
                pool.wait_ge(rope_done, layer * NQK + (NQK + 1))
                stage(layer, 0)
                with pool.Fori(1, HEADS - 1) as h:
                    pool.wait_ge(scores_done, layer * HEADS + h)
                    stage(layer, h)
                    head_rms(layer, h - 1)
                pool.wait_ge(scores_done, layer * HEADS + (HEADS - 1))
                stage(layer, HEADS - 1)
                gate(layer, 0)
                head_rms(layer, HEADS - 2)
                gate(layer, 1)
                head_rms(layer, HEADS - 1)
                rms(layer * 2 + 1)
            rms(2 * DEPTH)

        @block.scalar
        def _(act):
            def split(blk, first, last):
                for k in range(first, last):
                    if k % 2 == 0:
                        act.wait_ge(raw_landed[blk.raw_slot(k)], blk.landed(k))
                    if k < 2:
                        act.wait_ge(unit_released, blk.released + (k - 1))
                    elif k < NSPLIT:
                        act.wait_ge(tile_done, blk.tile0)
                    else:
                        act.wait_ge(unit_released, blk.released + (k - NSPLIT + 1))
                    act.activation(whi[:, blk.slot(k)], raw[:, blk.raw_slot(k), k % 2 * UNIT_KT:(k % 2 + 1) * UNIT_KT, :],
                                   ACT.Copy).then_inc(hi_ready, 1)

            def low_halves(blk, ev_free=None):
                if ev_free is not None:
                    act.wait_ge(ev_free[0], ev_free[1])
                for j in range(BT):
                    act.wait_ge(tile_done, blk.tile0 + (j + 1))
                    act.activation(ev[:, j, :], bank[j][:, S:2 * S], ACT.Copy).then_inc(low_copied, 1)

            def normed(tile, j, gain):
                constants_set(act)
                act.activation(xg[:, ds(tile, 1), 0:S], resid[:, ds(tile, 1), :], ACT.Copy,
                               scale=consts[:, ds(gain, 1)]).then_inc(xg_hi, 1)
                act.activation(ev[:, j, :].unsqueeze(1), resid[:, ds(tile, 1), :], ACT.Square).then_inc(squared, 1)

            def residual(layer, c, ffn):
                for j in range(BT):
                    act.wait_ge(x_updated, layer * (2 * KT) + (c * BT + (0 if ffn else KT) + j + 1))
                    normed(c * BT + j, j, layer * KT + (c * BT + j + (C_FFN if ffn else C_MIX + KT)))

            def conv(layer, u):
                for j in range(BT):
                    act.wait_ge(z_ready, layer * CT + (BT * u + j + 1))
                    constants_set(act)
                    act.activation(ev[:, j, :], gates[:, CT + BT * u + j, :], ACT.Copy,
                                   scale=consts[:, ds(layer * (3 * CT) + (C_CONV + CT + BT * u + j), 1)]
                                   ).then_inc(conv_mid, 1)

            def conv_out(layer, u):
                for j in range(BT):
                    act.wait_ge(gated, layer * CT + (BT * u + j + 1))
                    act.activation(mixed[:, HEADS + BT * u + j, 0:S], ev[:, j, :], ACT.Copy).then_inc(conv_hi, 1)

            def silu(layer, g):
                for j in range(2):
                    act.wait_ge(gate_scaled, layer * FT + (g * 2 + j + 1))
                    act.activation(ev[:, 2 * j, :], ev[:, 2 * j, :], ACT.Silu).then_inc(silu_done, 1)

            def hidden_out(layer, g):
                for j in range(2):
                    act.wait_ge(hidden_f32, layer * FT + (g * 2 + j + 1))
                    constants_set(act)
                    act.activation(hidden[:, ds(g * 2 + j, 1), 0:S], ev[:, 2 * j + 1, :].unsqueeze(1), ACT.Copy
                                   ).then_inc(hidden_hi, 1)

            def exps(layer, h):
                act.wait_ge(max_ready, layer * (2 * HEADS) + (h * 2 + 2))
                for m in range(2):
                    for q in range(QT):
                        c = m * QT + q
                        last = act.activation(probs[:, m, q, :], SCORE[m][:, S * q:S * (q + 1)], ACT.Exp,
                                              bias=neg_max[:, c:c + 1], accum_out=exp_sum[:, c:c + 1])
                last.then_inc(probs_done, 1)

            def copy_weights(layer, h):
                act.wait_ge(turned, layer * HEADS + (h + 1))
                act.activation(wt[:].rearrange("p k q -> p (k q)"), TURN[:], ACT.Copy).then_inc(wt_copied, 1)

            def head_squares(layer, h):
                act.wait_ge(heads_mixed, layer * HEADS + (h + 1))
                for q in range(QT):
                    last = act.activation(o_tok[:, q, :], MIX[:, P * q:P * (q + 1)], ACT.Square,
                                          accum_out=o_sq[:, q:q + 1])
                last.then_inc(o_squared, 1)

            def head_out(layer, h):
                constants_set(act)
                act.wait_ge(heads_turned, layer * HEADS + (h + 1))
                act.activation(mixed[:, ds(h, 1), 0:S], MIX[:, S:2 * S].unsqueeze(1), ACT.Copy,
                               scale=sub_gain[:, ds(layer, 1)]).then_inc(o_hi, 1)

            def sq_added_at(layer, norm, c):
                return layer * (2 * (KT + 1)) + (c * BT + norm * (KT + 1) + 1)

            act.wait_ge(lam_step, 2)
            act.activation(lam_exp[:], lam_sum[:], ACT.Exp).then_inc(lam_exped, 1)
            for t in range(KT):
                act.wait_ge(bank_free, t + 1)
                if t >= BT:
                    act.wait_ge(sq_added, t - BT + 2)
                normed(t, t % BT, C_MIX + t)

            with act.Fori(0, DEPTH) as layer:
                act.wait_ge(tile_done, layer * TILES_LAYER + PRE)
                constants_set(act)
                act.dma_start(cos_r[:], tables_d[0]).then_inc(tables_landed, 16)
                act.dma_start(sin_r[:], tables_d[1]).then_inc(tables_landed, 16)
                blk = Place(layer, 0)
                split(blk, 0, UNITS)
                prev = Place(layer, 0)
                blk = Place(layer, 1)
                split(blk, 0, 2)
                low_halves(prev, (sq_added, sq_added_at(layer, 0, NOUT)))
                split(blk, 2, UNITS)
                with act.Fori(2, NQK) as b:
                    blk = EarlyPlace(layer, b)
                    split(blk, 0, 2)
                    low_halves(EarlyPlace(layer, b - 1))
                    split(blk, 2, UNITS)
                blk = Place(layer, V0)
                split(blk, 0, 2)
                low_halves(Place(layer, V0 - 1))
                split(blk, 2, UNITS)
                exps(layer, 0)
                blk = Place(layer, V0 + 1)
                split(blk, 0, 6)
                copy_weights(layer, 0)
                head_squares(layer, 0)
                split(blk, 6, 7)
                exps(layer, 1)
                head_out(layer, 0)
                split(blk, 7, UNITS)

                def conv_block(b, ev_free, finish=None):
                    h = b - V0
                    blk = Place(layer, b)
                    split(blk, 0, 2)
                    copy_weights(layer, h - 1)
                    if ev_free is not False:
                        low_halves(Place(layer, b - 1), ev_free)
                    split(blk, 2, 4)
                    if finish is not None:
                        conv(layer, finish)
                    split(blk, 4, 6)
                    head_squares(layer, h - 1)
                    split(blk, 6, 7)
                    if finish is not None:
                        conv_out(layer, finish)
                    exps(layer, h)
                    head_out(layer, h - 1)
                    split(blk, 7, UNITS)

                conv_block(B0, False)
                conv_block(B0 + 1, None)
                with act.Fori(C0, U0 + 1) as b:
                    conv_block(b, (gate_stored, layer * (2 * CT) + (b * BT - C0 * BT + BT)))
                conv_block(U0 + 1, (gate_stored, layer * (2 * CT) + 2 * CT), finish=0)

                blk = Place(layer, OUT0)
                split(blk, 0, 2)
                copy_weights(layer, HEADS - 1)
                low_halves(Place(layer, OUT0 - 1), (conv_ready, layer * CT + BT))
                split(blk, 2, 4)
                conv(layer, 1)
                split(blk, 4, 6)
                head_squares(layer, HEADS - 1)
                conv_out(layer, 1)
                split(blk, 6, 7)
                head_out(layer, HEADS - 1)
                split(blk, 7, UNITS)
                blk = Place(layer, OUT0 + 1)
                split(blk, 0, 2)
                low_halves(Place(layer, OUT0), (conv_ready, layer * CT + CT))
                split(blk, 2, 4)
                residual(layer, 0, True)
                split(blk, 4, UNITS)
                with act.Fori(2, NOUT + 1) as c:
                    blk = Place(layer, c + OUT0)
                    split(blk, 0, 2)
                    low_halves(Place(layer, c + (OUT0 - 1)), (sq_added, sq_added_at(layer, 1, c - 1)))
                    split(blk, 2, 4)
                    residual(layer, c - 1, True)
                    split(blk, 4, UNITS)
                blk = Place(layer, GU0 + 1)
                split(blk, 0, 2)
                low_halves(Place(layer, GU0), (sq_added, sq_added_at(layer, 1, NOUT)))
                split(blk, 2, 4)
                silu(layer, 0)
                split(blk, 4, 5)
                hidden_out(layer, 0)
                split(blk, 5, UNITS)
                with act.Fori(2, NGU) as g:
                    blk = Place(layer, g + GU0)
                    split(blk, 0, 2)
                    low_halves(Place(layer, g + (GU0 - 1)), (hidden_ready, layer * FT + (g * 2 - 2)))
                    split(blk, 2, 4)
                    silu(layer, g - 1)
                    split(blk, 4, 5)
                    hidden_out(layer, g - 1)
                    split(blk, 5, UNITS)
                for d in range(NDOWN):
                    blk = Place(layer, None, down=d)
                    split(blk, 0, 2)
                    if d == 0:
                        low_halves(Place(layer, DOWN0 - 1), (hidden_ready, layer * FT + (FT - 2)))
                        split(blk, 2, 4)
                        silu(layer, NGU - 1)
                        split(blk, 4, 5)
                        hidden_out(layer, NGU - 1)
                        split(blk, 5, DUNITS)
                    else:
                        ev_free = ((hidden_ready, layer * FT + FT) if d == 1
                                   else (sq_added, sq_added_at(layer, 2, d - 1)))
                        low_halves(Place(layer, None, down=d - 1), ev_free)
                        split(blk, 2, 4)
                        residual(layer, d - 1, False)
                        split(blk, 4, DUNITS)
                low_halves(Place(layer, None, down=NDOWN - 1), (sq_added, sq_added_at(layer, 2, NDOWN - 1)))
                residual(layer, NDOWN - 1, False)

        @block.vector
        def _(dve):
            def split(blk, first, last):
                for k in range(first, last):
                    dve.wait_ge(hi_ready, blk.unit0 + (k + 1))
                    dve.tensor_tensor(wlo[:, blk.slot(k)], raw[:, blk.raw_slot(k), k % 2 * UNIT_KT:(k % 2 + 1) * UNIT_KT, :],
                                      lo_bits(whi[:, blk.slot(k)]), ALU.subtract).then_inc(weights_ready, 1)

            def sums(blk, qk_block=None):
                for j in range(BT):
                    dve.wait_ge(low_copied, blk.low0 + (j + 1))
                    if qk_block is None:
                        dst = ev[:, j, :]
                        dve.tensor_tensor(dst, bank[j][:, 0:S], ev[:, j, :], ALU.add).then_inc(bank_free, 1)
                    else:
                        dst = qk[:, ds(qk_block * BT + j, 1), :]
                        dve.tensor_tensor(dst, bank[j][:, 0:S].unsqueeze(1), ev[:, j, :].unsqueeze(1), ALU.add
                                          ).then_inc(bank_free, 1)

            def rotate(layer, c):
                tiles = qk[:, ds(c * BT, BT), :]
                dve.wait_ge(tables_ready, layer * 3 + 3)
                dve.wait_ge(swap_landed, layer * (64 * NQK) + (c * 64 + 64))
                dve.tensor_tensor(swapped[:], swapped[:], over_tiles(sin_r[:]), ALU.mult).then_inc(rope_step, 1)
                dve.tensor_tensor(tiles, tiles, over_tiles(cos_r[:]), ALU.mult).then_inc(rope_step, 1)
                dve.wait_ge(rope_step, layer * (2 * NQK) + (c * 2 + 2))
                dve.tensor_tensor(tiles, tiles, swapped[:], ALU.add).then_inc(rope_done, 1)

            def norm_sums(norm):
                dve.wait_ge(squares_summed, norm + 1)
                dve.tensor_scalar(mean_sq[:], MIX[:, 0:QT], 1.0 / DM, EPS, ALU.mult, ALU.add).then_inc(ms_ready, 1)
                dve.memset(sqacc[:], 0.0).then_inc(sq_added, 1)

            def norm_spread(norm):
                dve.wait_ge(rms_spread, norm + 1)
                dve.tensor_copy(rms_bc[:], MIX[:, S:2 * S]).then_inc(rms_copied, 1)

            def v_out(layer, i):
                blk = Place(layer, V0 + i)
                dve.wait_ge(rms_ready, layer * 2 + 1)
                for q in range(QT):
                    dve.wait_ge(tile_done, blk.tile0 + (q + 1))
                    dve.tensor_scalar(v_tok[:, q, COLS * i:COLS * (i + 1)], bank[QT * i + q][:], rms_tok[:, q:q + 1],
                                      None, ALU.mult).then_inc(bank_free, 1)

            def gate_out(layer, g, scale):
                for j in range(BT):
                    dve.wait_ge(bank_free, layer * TILES_LAYER
                                + (g * BT + PRE + BT * B0 - NV * (BT - QT) + j + 1))
                    dve.tensor_tensor(gates[:, ds(g * BT + j, 1), :], ev[:, j, :].unsqueeze(1), scale[:].unsqueeze(1),
                                      ALU.mult).then_inc(gate_stored, 1)

            def conv_products(layer, u):
                dve.wait_ge(gate_stored, layer * (2 * CT) + 2 * CT)
                for j in range(BT):
                    t = CT + BT * u + j
                    dve.wait_ge(bank_free, Place(layer, U0 + u).tile0 + (j + 1))
                    dve.tensor_tensor(gates[:, t, :], ev[:, j, :], gates[:, t, :], ALU.mult).then_inc(z_ready, 1)

            def conv_neighbours(layer, u):
                for side in range(2):
                    for j in range(BT):
                        t = CT + BT * u + j
                        tap = consts[:, ds(layer * (3 * CT) + (C_CONV + 2 * side * CT + BT * u + j), 1)]
                        step = layer * (2 * CT) + (2 * BT * u + j)
                        if side == 0:
                            dve.wait_ge(conv_mid, layer * CT + (BT * u + j + 1))
                            to, frm = ev[:, j, 1:S], gates[:, t, 0:S - 1]
                        else:
                            dve.wait_ge(conv_step, step + 1)
                            to, frm = ev[:, j, 0:S - 1], gates[:, t, 1:S]
                        dve.scalar_tensor_tensor(to, frm, tap, to, ALU.mult, ALU.add).then_inc(conv_step, 1)

            def conv_low(layer, u):
                for j in range(BT):
                    dve.wait_ge(conv_hi, layer * CT + (BT * u + j + 1))
                    t = HEADS + BT * u + j
                    dve.tensor_tensor(mixed[:, t, S:2 * S], ev[:, j, :], lo_bits(mixed[:, t, 0:S]), ALU.subtract
                                      ).then_inc(conv_ready, 1)

            def row_max(layer, h):
                dve.wait_ge(scores_done, layer * HEADS + (h + 1))
                for m in range(2):
                    dve.reduce_max(neg_max[:, QT * m:QT * (m + 1)], SCORE[m][:].rearrange("p (q k) -> p q k", q=QT),
                                   AX_X, negate=True).then_inc(max_ready, 1)

            def combine(layer, h):
                step = layer * (6 * HEADS) + h * 6
                dve.wait_ge(probs_done, layer * HEADS + (h + 1))
                dve.reciprocal(exp_inv[:], exp_sum[:]).then_inc(w_step, 1)
                dve.wait_ge(w_step, step + 1)
                dve.tensor_scalar(exp_inv[:, QT:2 * QT], exp_inv[:, QT:2 * QT], neg_lam[:, ds(layer, 1)], None,
                                  ALU.mult).then_inc(w_step, 1)
                for q in range(QT):
                    dve.tensor_scalar(probs[:, 0, q, :], probs[:, 0, q, :], exp_inv[:, q:q + 1], None,
                                      ALU.mult).then_inc(w_step, 1)
                for q in range(QT):
                    dve.wait_ge(w_step, step + (3 + q))
                    dve.scalar_tensor_tensor(probs[:, 0, q, :], probs[:, 1, q, :], exp_inv[:, QT + q:QT + q + 1],
                                             probs[:, 0, q, :], ALU.mult, ALU.add).then_inc(w_step, 1)

            def head_scale(layer, h):
                dve.wait_ge(o_rms_ready, layer * HEADS + (h + 1))
                for q in range(QT):
                    dve.tensor_scalar(o_tok[:, q, :], MIX[:, P * q:P * (q + 1)], o_rms[:, q:q + 1], None,
                                      ALU.mult).then_inc(o_scaled, 1)

            def head_low(layer, h):
                dve.wait_ge(o_hi, layer * HEADS + (h + 1))
                dve.scalar_tensor_tensor(mixed[:, ds(h, 1), S:2 * S], MIX[:, S:2 * S].unsqueeze(1),
                                         sub_gain[:, ds(layer, 1)], lo_bits(mixed[:, ds(h, 1), 0:S]),
                                         ALU.mult, ALU.subtract).then_inc(o_ready, 1)

            def add_residual(layer, c, blk):
                for j in range(BT):
                    dve.wait_ge(bank_free, blk.tile0 + (j + 1))
                    t = resid[:, ds(c * BT + j, 1), :]
                    dve.tensor_tensor(t, t, ev[:, j, :].unsqueeze(1), ALU.add).then_inc(x_updated, 1)

            def normed_low(norm, tile, j, gain):
                dve.wait_ge(xg_hi, norm * KT + (tile + 1))
                dve.scalar_tensor_tensor(xg[:, ds(tile, 1), S:2 * S], resid[:, ds(tile, 1), :], consts[:, ds(gain, 1)],
                                         lo_bits(xg[:, ds(tile, 1), 0:S]), ALU.mult, ALU.subtract
                                         ).then_inc(xg_ready, 1)
                dve.wait_ge(squared, norm * KT + (tile + 1))
                dve.wait_ge(sq_added, norm * (KT + 1) + (tile + 1))
                dve.tensor_tensor(sqacc[:], sqacc[:], ev[:, j, :], ALU.add).then_inc(sq_added, 1)

            def residual_low(layer, c, ffn):
                for j in range(BT):
                    normed_low(layer * 2 + (1 if ffn else 2), c * BT + j, j,
                               layer * KT + (c * BT + j + (C_FFN if ffn else C_MIX + KT)))

            def scale_gu(layer, g, blk):
                dve.wait_ge(rms_copied, layer * 2 + 2)
                for j in range(2):
                    for tile, done in ((2 * j, gate_scaled), (2 * j + 1, up_scaled)):
                        dve.wait_ge(bank_free, blk.tile0 + (tile + 1))
                        dve.tensor_tensor(ev[:, tile, :], ev[:, tile, :], rms_bc[:], ALU.mult).then_inc(done, 1)

            def hidden_products(layer, g):
                for j in range(2):
                    n = layer * FT + (g * 2 + j + 1)
                    dve.wait_ge(silu_done, n)
                    dve.wait_ge(up_scaled, n)
                    dve.tensor_tensor(ev[:, 2 * j + 1, :], ev[:, 2 * j + 1, :], ev[:, 2 * j, :], ALU.mult
                                      ).then_inc(hidden_f32, 1)

            def hidden_low(layer, g):
                for j in range(2):
                    dve.wait_ge(hidden_hi, layer * FT + (g * 2 + j + 1))
                    t = ds(g * 2 + j, 1)
                    dve.tensor_tensor(hidden[:, t, S:2 * S], ev[:, 2 * j + 1, :].unsqueeze(1),
                                      lo_bits(hidden[:, t, 0:S]), ALU.subtract).then_inc(hidden_ready, 1)

            dve.memset(ones[:], 1.0).then_inc(weights_ready, SPLIT_BIAS)
            dve.memset(neg_half[:], -0.5).then_inc(set_up, 1)
            dve.memset(q_scale[:], HD ** -0.5).then_inc(set_up, 1)
            dve.memset(inv_width[:], 1.0 / (2 * HD)).then_inc(set_up, 1)
            dve.memset(eps[:], EPS).then_inc(rope_done, 1)
            dve.memset(sqacc[:], 0.0).then_inc(sq_added, 1)
            dve.wait_ge(small_landed, 48)
            dve.tensor_tensor(lam_prod[:].rearrange("p (l m) d -> p l m d", l=DEPTH), lambdas[:, :, :, 0, :],
                              lambdas[:, :, :, 1, :], ALU.mult).then_inc(lam_step, 1)
            dve.wait_ge(lam_step, 1)
            dve.reduce_sum(lam_sum[:], lam_prod[:], AX_X).then_inc(lam_step, 1)
            for l in range(DEPTH):
                lam_init = 0.8 - 0.6 * math.exp(-0.3 * l)
                dve.tensor_scalar(sub_gain[:, l:l + 1], consts[:, C_SUB + l:C_SUB + l + 1], 1.0 - lam_init, None,
                                  ALU.mult)
            dve.wait_ge(lam_exped, 1)
            for l in range(DEPTH):
                dve.tensor_tensor(lam_dif[:, l:l + 1], lam_exp[:, 2 * l + 1:2 * l + 2], lam_exp[:, 2 * l:2 * l + 1],
                                  ALU.subtract).then_inc(lam_step, 1)
            for l in range(DEPTH):
                lam_init = 0.8 - 0.6 * math.exp(-0.3 * l)
                dve.wait_ge(lam_step, 3 + l)
                last = dve.tensor_scalar(neg_lam[:, l:l + 1], lam_dif[:, l:l + 1], lam_init, None, ALU.subtract)
            last.then_inc(set_up, 1)
            for t0 in range(0, KT, BT):
                for j in range(BT):
                    dve.wait_ge(tile_done, t0 + j + 1)
                    dve.tensor_copy(resid[:, t0 + j, :], bank[j][:, 0:S]).then_inc(bank_free, 1)
                for j in range(BT):
                    normed_low(0, t0 + j, j, C_MIX + t0 + j)

            with dve.Fori(0, DEPTH) as layer:
                blk = Place(layer, 0)
                split(blk, 0, 7)
                norm_sums(layer * 2)
                split(blk, 7, UNITS)
                norm_spread(layer * 2)
                dve.wait_ge(tables_landed, layer * 32 + 32)
                dve.wait_ge(rms_copied, layer * 2 + 1)
                dve.tensor_tensor(cos_r[:], cos_r[:], rms_bc[:], ALU.mult).then_inc(tables_ready, 1)
                dve.tensor_tensor(sin_r[:], sin_r[:], rms_bc[:], ALU.mult).then_inc(tables_ready, 1)
                dve.tensor_tensor(rms2_bc[:], rms_bc[:], rms_bc[:], ALU.mult).then_inc(tables_ready, 1)
                with dve.Fori(1, NQK) as b:
                    blk = EarlyPlace(layer, b)
                    split(blk, 0, 2)
                    sums(EarlyPlace(layer, b - 1), b - 1)
                    split(blk, 2, 6)
                    rotate(layer, b - 1)
                    split(blk, 6, UNITS)
                blk = Place(layer, V0)
                split(blk, 0, 2)
                sums(Place(layer, V0 - 1), NQK - 1)
                split(blk, 2, 5)
                rotate(layer, NQK - 1)
                split(blk, 5, UNITS)
                row_max(layer, 0)
                blk = Place(layer, V0 + 1)
                split(blk, 0, 2)
                combine(layer, 0)
                v_out(layer, 0)
                split(blk, 2, 6)
                row_max(layer, 1)
                head_scale(layer, 0)
                split(blk, 6, 7)
                combine(layer, 1)
                split(blk, 7, UNITS)
                head_low(layer, 0)

                def attention_part(blk, h):
                    split(blk, 4, 6)
                    head_scale(layer, h - 1)
                    row_max(layer, h)
                    split(blk, 6, 7)
                    combine(layer, h)
                    split(blk, 7, UNITS)
                    head_low(layer, h - 1)

                blk = Place(layer, B0)
                split(blk, 0, 2)
                v_out(layer, 1)
                split(blk, 2, 4)
                attention_part(blk, 2)
                for kind, scale in ((0, rms_bc), (1, rms2_bc)):
                    with dve.Fori(kind * NG, (kind + 1) * NG) as g:
                        blk = Place(layer, g + (B0 + 1))
                        split(blk, 0, 2)
                        sums(Place(layer, g + B0))
                        split(blk, 2, 3)
                        gate_out(layer, g, scale)
                        split(blk, 3, 4)
                        attention_part(blk, g + 3)
                blk = Place(layer, U0 + 1)
                split(blk, 0, 2)
                sums(Place(layer, U0))
                split(blk, 2, 3)
                conv_products(layer, 0)
                split(blk, 3, 4)
                conv_neighbours(layer, 0)
                split(blk, 4, 6)
                head_scale(layer, HEADS - 2)
                row_max(layer, HEADS - 1)
                split(blk, 6, 7)
                conv_low(layer, 0)
                combine(layer, HEADS - 1)
                split(blk, 7, UNITS)
                head_low(layer, HEADS - 2)
                blk = Place(layer, OUT0)
                split(blk, 0, 2)
                sums(Place(layer, U0 + 1))
                split(blk, 2, 3)
                conv_products(layer, 1)
                split(blk, 3, 4)
                conv_neighbours(layer, 1)
                split(blk, 4, 6)
                head_scale(layer, HEADS - 1)
                conv_low(layer, 1)
                split(blk, 6, 7)
                head_low(layer, HEADS - 1)
                split(blk, 7, UNITS)
                with dve.Fori(1, NOUT) as c:
                    blk = Place(layer, c + OUT0)
                    prev = Place(layer, c + (OUT0 - 1))
                    split(blk, 0, 2)
                    sums(prev)
                    split(blk, 2, 3)
                    add_residual(layer, c - 1, prev)
                    split(blk, 3, 4)
                    residual_low(layer, c - 1, True)
                    split(blk, 4, UNITS)
                blk = Place(layer, GU0)
                prev = Place(layer, GU0 - 1)
                split(blk, 0, 2)
                sums(prev)
                split(blk, 2, 3)
                add_residual(layer, NOUT - 1, prev)
                split(blk, 3, 4)
                residual_low(layer, NOUT - 1, True)
                split(blk, 4, 7)
                norm_sums(layer * 2 + 1)
                split(blk, 7, UNITS)
                norm_spread(layer * 2 + 1)
                with dve.Fori(1, NGU) as g:
                    blk = Place(layer, g + GU0)
                    prev = Place(layer, g + (GU0 - 1))
                    split(blk, 0, 2)
                    sums(prev)
                    split(blk, 2, 3)
                    scale_gu(layer, g - 1, prev)
                    split(blk, 3, 4)
                    hidden_products(layer, g - 1)
                    split(blk, 4, 5)
                    hidden_low(layer, g - 1)
                    split(blk, 5, UNITS)
                for d in range(NDOWN):
                    blk = Place(layer, None, down=d)
                    split(blk, 0, 2)
                    if d == 0:
                        prev = Place(layer, DOWN0 - 1)
                        sums(prev)
                        split(blk, 2, 3)
                        scale_gu(layer, NGU - 1, prev)
                        split(blk, 3, 4)
                        hidden_products(layer, NGU - 1)
                        split(blk, 4, 5)
                        hidden_low(layer, NGU - 1)
                        split(blk, 5, DUNITS)
                    else:
                        prev = Place(layer, None, down=d - 1)
                        sums(prev)
                        split(blk, 2, 3)
                        add_residual(layer, d - 1, prev)
                        split(blk, 3, 4)
                        residual_low(layer, d - 1, False)
                        split(blk, 4, DUNITS)
                prev = Place(layer, None, down=NDOWN - 1)
                sums(prev)
                add_residual(layer, NDOWN - 1, prev)
                residual_low(layer, NDOWN - 1, False)

            dve.wait_ge(x_updated, 2 * KT * DEPTH)
            for t in range(KT):
                dve.tensor_scalar(resid[:, t, :], resid[:, t, :], consts[:, C_FIN + t:C_FIN + t + 1], None,
                                  ALU.mult).then_inc(out_scaled, 1)
            norm_sums(2 * DEPTH)
            dve.wait_ge(rms_ready, 2 * DEPTH + 1)
            for g in range(QT * BT):
                q, c = divmod(g, BT)
                dve.wait_ge(tile_done, PRE + DEPTH * TILES_LAYER + g + 1)
                dve.tensor_scalar(x_tok[:, q, COLS * c:COLS * (c + 1)], bank[g % 4][:], rms_tok[:, q:q + 1], None,
                                  ALU.mult).then_inc(out_ready, 1)

        @block.tensor
        def _(pe):
            def unit_releasedy(blk, k):
                pe.wait_ge(weights_ready, blk.unit0 + (SPLIT_BIAS + k + 1))

            def products(blk, ks, moving, kts=range(FT), cols=PLAIN):
                for k in ks:
                    unit_releasedy(blk, k)
                for j in range(BT):
                    if ks[0] == 0:
                        pe.wait_ge(bank_free, blk.tile0 + (j + 1 - BT))
                    for k in ks:
                        for i in range(UNIT_KT):
                            kt = kts[UNIT_KT * k + i]
                            w = slice(P * cols[j], P * (cols[j] + 1))
                            pe.matmul(bank[j][:], whi[:, blk.slot(k), i, w], moving[:, kt, :],
                                      start=(k == 0 and i == 0), stop=False, skip_group_check=True)
                            last = pe.matmul(bank[j][:, 0:S], wlo[:, blk.slot(k), i, w], moving[:, kt, 0:S],
                                             start=False, stop=(k == blk.units - 1 and i == UNIT_KT - 1),
                                             skip_group_check=True)
                        if j == BT - 1 and k < blk.units - 2:
                            last.then_inc(unit_released, 1)
                    if ks[-1] == blk.units - 1:
                        last.then_inc(tile_done, 1)

            def v_products(blk, i, ks):
                for k in ks:
                    unit_releasedy(blk, k)
                for q in range(QT):
                    b = bank[QT * i + q]
                    if ks[0] == 0:
                        pe.wait_ge(bank_free, blk.tile0 + (q + 1 - BT))
                    for k in ks:
                        for r in range(UNIT_KT):
                            kt = UNIT_KT * k + r
                            x_hi = xg[:, kt, P * q:P * (q + 1)]
                            x_lo = xg[:, kt, S + P * q:S + P * (q + 1)]
                            w_hi, w_lo = whi[:, blk.slot(k), r, :], wlo[:, blk.slot(k), r, :]
                            final = k == blk.units - 1 and r == UNIT_KT - 1
                            pe.matmul(b[:], x_hi, w_hi, start=(k == 0 and r == 0), stop=False)
                            pe.matmul(b[:], x_hi, w_lo, start=False, stop=False)
                            last = pe.matmul(b[:], x_lo, w_hi, start=False, stop=final)
                        if q == QT - 1 and k < blk.units - 2:
                            last.then_inc(unit_released, 1)
                    if ks[-1] == blk.units - 1:
                        last.then_inc(tile_done, 1)

            def sum_squares(norm):
                pe.wait_ge(sq_added, norm * (KT + 1) + (KT + 1))
                for q in range(QT):
                    last = pe.matmul(MIX[:, q:q + 1], sqacc[:, P * q:P * (q + 1)], ones[:], start=True, stop=True)
                last.then_inc(squares_summed, 1)

            def spread_rms(norm):
                pe.wait_ge(rms_ready, norm + 1)
                for q in range(QT):
                    last = pe.matmul(MIX[:, S + P * q:S + P * (q + 1)], rms_tok[:, q:q + 1].to_broadcast([P, P]), ident[:],
                                     start=True, stop=True)
                last.then_inc(rms_spread, 1)

            def scores(layer, h):
                pe.wait_ge(staged, layer * HEADS + (h + 1))
                if not isinstance(h, int) or h > 0:
                    pe.wait_ge(probs_done, layer * HEADS + h)
                for q in range(QT):
                    for m in range(2):
                        rows = slice(HD * m, HD * (m + 1))
                        last = pe.matmul(SCORE[m][:, S * q:S * (q + 1)], q_head[rows, P * q:P * (q + 1)], k_head[rows, :],
                                         start=True, stop=True)
                last.then_inc(scores_done, 1)

            def turn_weights(layer, h):
                pe.wait_ge(w_step, layer * (6 * HEADS) + (h * 6 + 6))
                for k in range(QT):
                    for q in range(QT):
                        last = pe.transpose(TURN[:, S * k + P * q:S * k + P * (q + 1)],
                                            probs[:, 0, q, P * k:P * (k + 1)], ident[:])
                last.then_inc(turned, 1)

            def mix(layer, h):
                pe.wait_ge(wt_copied, layer * HEADS + (h + 1))
                if isinstance(h, int) and h == 0:
                    pe.wait_ge(rms_copied, layer * 2 + 1)
                else:
                    pe.wait_ge(o_ready, layer * HEADS + h)
                for q in range(QT):
                    for k in range(QT):
                        last = pe.matmul(MIX[:, P * q:P * (q + 1)].unsqueeze(1), wt[:, k, P * q:P * (q + 1)],
                                         v_tok[:, k:k + 1, ds(h * P, P)], start=(k == 0), stop=(k == QT - 1))
                last.then_inc(heads_mixed, 1)

            def turn_head(layer, h):
                pe.wait_ge(o_scaled, layer * (QT * HEADS) + (h * QT + QT))
                for q in range(QT):
                    last = pe.transpose(MIX[:, S + P * q:S + P * (q + 1)], o_tok[:, q, :], ident[:])
                last.then_inc(heads_turned, 1)

            def first_block(blk, norm, cols):
                def tiles_ready(k):
                    pe.wait_ge(xg_ready, norm * KT + (UNIT_KT * k + UNIT_KT))

                tiles_ready(1)
                products(blk, [0, 1], xg, cols=cols)
                for k in range(2, UNITS - 2):
                    tiles_ready(k)
                    products(blk, [k], xg, cols=cols)
                    if k == 2:
                        sum_squares(norm)
                    if k == 4:
                        spread_rms(norm)
                tiles_ready(UNITS - 1)
                products(blk, [UNITS - 2, UNITS - 1], xg, cols=cols)

            pe.wait_ge(x_landed, 16)
            pe.wait_ge(small_landed, 48)
            for t in range(KT):
                if t >= BT:
                    pe.wait_ge(bank_free, t - BT + 1)
                for q in range(QT):
                    last = pe.transpose(bank[t % BT][:, P * q:P * (q + 1)], x_tok[:, q, P * t:P * (t + 1)], ident[:])
                    if t == 0 and q == 0:
                        last.then_inc(unit_released, RELEASE_BIAS)
                last.then_inc(tile_done, 1)

            with pe.Fori(0, DEPTH) as layer:
                first_block(Place(layer, 0), layer * 2, PLAIN)
                with pe.Fori(1, NQK) as b:
                    blk = EarlyPlace(layer, b)
                    products(blk, [0, 1], xg)
                    for k in range(2, UNITS - 2):
                        products(blk, [k], xg)
                    products(blk, [UNITS - 2, UNITS - 1], xg)
                blk = Place(layer, V0)
                v_products(blk, 0, [0, 1])
                for k in range(2, UNITS - 2):
                    v_products(blk, 0, [k])
                scores(layer, 0)
                v_products(blk, 0, [UNITS - 2, UNITS - 1])
                blk = Place(layer, V0 + 1)
                v_products(blk, 1, [0, 1])
                turn_weights(layer, 0)
                v_products(blk, 1, [2])
                pe.wait_ge(bank_free, blk.tile0)
                mix(layer, 0)
                v_products(blk, 1, [3])
                scores(layer, 1)
                v_products(blk, 1, [4])
                turn_head(layer, 0)
                v_products(blk, 1, [5])
                turn_weights(layer, 1)
                v_products(blk, 1, [6, 7])
                with pe.Fori(B0, OUT0) as b:
                    h = b - V0
                    blk = Place(layer, b)
                    products(blk, [0, 1], xg)
                    mix(layer, h - 1)
                    products(blk, [2], xg)
                    scores(layer, h)
                    products(blk, [3], xg)
                    turn_head(layer, h - 1)
                    products(blk, [4], xg)
                    products(blk, [5], xg)
                    turn_weights(layer, h)
                    products(blk, [6, 7], xg)
                blk = Place(layer, OUT0)
                pe.wait_ge(o_ready, layer * HEADS + (HEADS - 2))
                products(blk, [0, 1], mixed, OUT_ORDER)
                mix(layer, HEADS - 1)
                products(blk, [2], mixed, OUT_ORDER)
                pe.wait_ge(conv_ready, layer * CT + BT)
                products(blk, [3], mixed, OUT_ORDER)
                turn_head(layer, HEADS - 1)
                products(blk, [4], mixed, OUT_ORDER)
                pe.wait_ge(conv_ready, layer * CT + CT)
                products(blk, [5], mixed, OUT_ORDER)
                pe.wait_ge(o_ready, layer * HEADS + HEADS)
                products(blk, [6, 7], mixed, OUT_ORDER)
                with pe.Fori(1, NOUT) as c:
                    blk = Place(layer, c + OUT0)
                    products(blk, [0, 1], mixed, OUT_ORDER)
                    for k in range(2, UNITS - 2):
                        products(blk, [k], mixed, OUT_ORDER)
                    products(blk, [UNITS - 2, UNITS - 1], mixed, OUT_ORDER)
                first_block(Place(layer, GU0), layer * 2 + 1, GU_COLS)
                with pe.Fori(1, NGU) as g:
                    blk = Place(layer, g + GU0)
                    products(blk, [0, 1], xg, cols=GU_COLS)
                    for k in range(2, UNITS - 2):
                        products(blk, [k], xg, cols=GU_COLS)
                    products(blk, [UNITS - 2, UNITS - 1], xg, cols=GU_COLS)
                with pe.Fori(0, NDOWN // 2) as pair:
                    pe.wait_ge(hidden_ready, layer * FT + (FT - 2))
                    for half in range(2):
                        blk = Place(layer, None, down=half)
                        n = pair * 2
                        blk.unit0 = blk.unit0 + n * DUNITS
                        blk.tile0 = blk.tile0 + n * BT
                        products(blk, [0, 1], hidden)
                        for k in range(2, DUNITS - 2):
                            products(blk, [k], hidden)
                        if half == 0:
                            pe.wait_ge(hidden_ready, layer * FT + FT)
                        products(blk, [DUNITS - 2, DUNITS - 1], hidden)

            sum_squares(2 * DEPTH)
            pe.wait_ge(out_scaled, KT)
            for g in range(QT * BT):
                q, c = divmod(g, BT)
                if g < 4:
                    pe.wait_ge(bank_free, PRE + DEPTH * TILES_LAYER - BT + g + 1)
                else:
                    pe.wait_ge(out_ready, g - 4 + 1)
                for i in range(BT):
                    last = pe.transpose(bank[g % 4][:, P * i:P * (i + 1)], resid[:, BT * c + i, P * q:P * (q + 1)], ident[:])
                last.then_inc(tile_done, 1)


def kernel(x, norm_mix, w_in, lambda_q1, lambda_k1, lambda_q2, lambda_k2, subln, conv_w, w_out, norm_ffn,
           w_gate, w_up, w_down, norm_final):
    import concourse.bacc as bacc
    from concourse.bass_utils import run_bass_kernel_spmd

    arr = np.ascontiguousarray

    def tiled(v):
        v = np.asarray(v)
        return v.reshape(-1, P).T

    consts = arr(np.concatenate([tiled(norm_mix), tiled(norm_final), tiled(norm_ffn), tiled(conv_w), tiled(subln)],
                                axis=1))
    lam = np.stack([np.stack([np.asarray(lambda_q1), np.asarray(lambda_k1)], 1),
                    np.stack([np.asarray(lambda_q2), np.asarray(lambda_k2)], 1)], 1)
    lam = arr(np.broadcast_to(lam[None], (P,) + lam.shape))
    half = HD // 2
    inv = np.float32(THETA) ** (-np.arange(0, HD, 2, dtype=np.float32) / np.float32(HD))
    ang = np.arange(S, dtype=np.float32)[None, :] * inv[np.arange(P) % half][:, None]
    sign = np.where(np.arange(P) % HD < half, np.float32(-1), np.float32(1))[:, None]
    tables = arr(np.stack([np.cos(ang), np.sin(ang) * sign]).astype(np.float32))

    nc = bacc.Bacc("TRN2", target_bir_lowering=False, num_devices=1)
    ins = {"x": arr(x), "w_in": arr(w_in), "w_out": arr(w_out), "w_gate": arr(w_gate), "w_up": arr(w_up),
           "w_down": arr(w_down), "consts": consts, "lambdas": lam, "tables": tables,
           "ident": np.eye(P, dtype=np.float32)}
    args = [nc.dram_tensor(f"{n}_dram", a.shape, mybir.dt.from_np(a.dtype), kind="ExternalInput").ap()
            for n, a in ins.items()]
    out = nc.dram_tensor("out_dram", (1, S, DM), F32, kind="ExternalOutput").ap()
    build_program(nc, *args, out)
    r = run_bass_kernel_spmd(nc, [{f"{n}_dram": a for n, a in ins.items()}], core_ids=[0])
    return r.results[0]["out_dram"]
```

```python
import math

import numpy as np
from concourse import mybir
import concourse.bass as bass

F32 = mybir.dt.float32
F32R = mybir.dt.float32r
ALU = mybir.AluOpType
ACT = mybir.ActivationFunctionType
AX_X = mybir.AxisListType.X

P = 128
S = 256
QT = S // P
DM = 2048
DEPTH = 2
HEADS = 8
HD = 64
AW = HEADS * 2 * HD
CW = DM - AW
FF = -(-8 * DM // (3 * 256)) * 256
EPS = 1e-6
THETA = 10000.0
KT = DM // P
FT = FF // P
CT = CW // P
COLS = 512
BT = COLS // P
UNIT_KT = 2
LOAD_KT = 2 * UNIT_KT
NRAW = 4
NSPLIT = 4

NQK = 2 * AW // COLS
NV = AW // COLS
NG = CW // COLS
NOUT = DM // COLS
NGU = 2 * FF // COLS
NDOWN = DM // COLS
V0 = NQK
B0 = V0 + NV
C0 = B0 + NG
U0 = C0 + NG
OUT0 = U0 + NG
GU0 = OUT0 + NOUT
DOWN0 = GU0 + NGU
UNITS = KT // UNIT_KT
DUNITS = FT // UNIT_KT
LOADS = UNITS // 2
DLOADS = DUNITS // 2
UNITS_LAYER = DOWN0 * UNITS + NDOWN * DUNITS
TILES_LAYER = BT * (DOWN0 + NDOWN) - NV * (BT - QT)
RELEASES_LAYER = DOWN0 * (UNITS - 2) + NDOWN * (DUNITS - 2)
LOW_LAYER = BT * (DOWN0 + NDOWN - NV)
PRE = KT
EARLY_TILES = PRE - BT
SQ_STEPS = 4 * (EARLY_TILES // BT)
SPLIT_BIAS = 2 * NRAW
RELEASE_BIAS = 2
PAIR_USES = [len(range(s, 2 * DLOADS, NRAW)) for s in range(NRAW)]
LAYER_USES = [DOWN0 + NDOWN // 2 * PAIR_USES[s] for s in range(NRAW)]
OUT_ORDER = [0, 1, 2, 3, 4, 5, 8, 9, 10, 11, 12, 13, 14, 15, 6, 7]
OUT_BANKS = [4, 5, 6, 0, 1, 2, 3, 4]
GU_COLS = [0, 2, 1, 3]
PLAIN = [0, 1, 2, 3]

C_MIX = 0
C_FIN = C_MIX + DEPTH * KT
C_FFN = C_FIN + KT
C_CONV = C_FFN + DEPTH * KT
C_SUB = C_CONV + DEPTH * 3 * CT
N_CONST = C_SUB + DEPTH


def x_bank(t):
    return (t + BT) % (2 * BT)


class Place:

    def __init__(self, layer, b, down=None):
        self.down = down
        self.layer = layer
        if down is None:
            self.units = UNITS
            early = isinstance(b, int) and b < B0
            tiles = (BT * b if b <= V0 else BT * V0 + QT * (b - V0)) if early else BT * b - NV * (BT - QT)
            self.unit0 = layer * UNITS_LAYER + b * UNITS
            self.released = layer * RELEASES_LAYER + (b * (UNITS - 2) + RELEASE_BIAS)
            low = b if early else b - NV
            self.slot0 = 0
            self.load0 = 0
            self.b = b
        else:
            self.units = DUNITS
            tiles = BT * (DOWN0 + down) - NV * (BT - QT)
            self.unit0 = layer * UNITS_LAYER + (down * DUNITS + DOWN0 * UNITS)
            self.released = layer * RELEASES_LAYER + (down * (DUNITS - 2) + DOWN0 * (UNITS - 2) + RELEASE_BIAS)
            low = DOWN0 + down - NV
            self.slot0 = down % 2 * DUNITS % NSPLIT
            self.load0 = down % 2 * DLOADS
        self.tile0 = layer * TILES_LAYER + (PRE + tiles)
        self.low0 = layer * LOW_LAYER + BT * (low + 1)

    def slot(self, k):
        return (self.slot0 + k) % NSPLIT

    def raw_slot(self, k):
        return (self.load0 + k // 2) % NRAW

    def landed(self, k):
        s = self.raw_slot(k)
        if self.down is None:
            return self.layer * (32 * LAYER_USES[s]) + (self.b * 32 + 32)
        n = DOWN0 + self.down // 2 * PAIR_USES[s] + (self.load0 + k // 2) // NRAW
        return self.layer * (32 * LAYER_USES[s]) + 32 * (n + 1)


class EarlyPlace(Place):

    def __init__(self, layer, b):
        Place.__init__(self, layer, b)
        self.tile0 = layer * TILES_LAYER + (b * BT + PRE)
        self.low0 = layer * LOW_LAYER + (b * BT + BT)


class LastPlace:

    def __init__(self, layer):
        self.tile0 = layer * TILES_LAYER + (PRE - BT)
        self.low0 = layer * LOW_LAYER


def build_program(nc, x, w_in, w_out, w_gate, w_up, w_down, consts_d, lambdas_d, tables_d, ident_d, out):
    start = -(-nc.sbuf_base // 32) * 32
    end = nc.sbuf_top
    place = [start]

    def at(name, shape, dtype, offset):
        return nc.alloc_sbuf_tensor_at(name, shape, dtype, offset=offset)

    def put(name, shape, dtype):
        offset = place[0]
        place[0] = offset + -(-int(np.prod(shape[1:])) * 4 // 32) * 32
        assert place[0] <= end, (name, place[0], end)
        return at(name, shape, dtype, offset)

    raw = put("raw", [P, NRAW, LOAD_KT, COLS], F32)
    whi = put("whi", [P, NSPLIT, UNIT_KT, COLS], F32R)
    wlo = put("wlo", [P, NSPLIT, UNIT_KT, COLS], F32R)
    resid = put("resid", [P, KT, S], F32)
    xg = put("xg", [P, KT, 2 * S], F32R)
    shared = place[0]
    hidden = put("hidden", [P, FT, 2 * S], F32R)
    shared_end = place[0]
    ev = put("ev", [P, BT, S], F32)
    sqacc = put("sqacc", [P, S], F32)
    rms_bc = put("rms_bc", [P, S], F32)
    consts = put("consts", [P, N_CONST], F32)
    ident = put("ident", [P, P], F32)
    ones = put("ones", [P, 1], F32)
    neg_half = put("neg_half", [P, QT], F32)
    inv_width = put("inv_width", [P, QT], F32)
    eps = put("eps", [P, QT], F32)
    q_scale = put("q_scale", [P, 1], F32)
    mean_sq = put("mean_sq", [P, QT], F32)
    rms_tok = put("rms_tok", [P, QT], F32)
    neg_lam = put("neg_lam", [P, DEPTH], F32)
    sub_gain = put("sub_gain", [P, DEPTH], F32)
    neg_max = put("neg_max", [P, 2 * QT], F32)
    exp_sum = put("exp_sum", [P, 2 * QT], F32)
    exp_inv = put("exp_inv", [P, 2 * QT], F32)
    o_sq = put("o_sq", [P, QT], F32)
    o_ms = put("o_ms", [P, QT], F32)
    o_rms = put("o_rms", [P, QT], F32)

    spot = [shared]

    def share(name, shape, dtype):
        offset = spot[0]
        spot[0] = offset + int(np.prod(shape[1:])) * 4
        assert spot[0] <= shared_end, name
        return at(name, shape, dtype, offset)

    qk = share("qk", [P, 2 * HEADS, S], F32)
    gates = share("gates", [P, 2 * CT, S], F32)
    v_tok = share("v_tok", [P, QT, AW], F32)
    mixed = share("mixed", [P, KT, 2 * S], F32R)
    swapped = share("swapped", [P, BT, S], F32)
    cos_r = share("cos_r", [P, S], F32)
    sin_r = share("sin_r", [P, S], F32)
    rms2_bc = share("rms2_bc", [P, S], F32)
    q_hi = share("q_hi", [P, S], F32R)
    k_hi = share("k_hi", [P, S], F32R)
    probs = share("probs", [P, 2, QT, S], F32)
    wt = share("wt", [P, QT, S], F32)
    o_tok = share("o_tok", [P, QT, P], F32)
    swapped_at = shared + 4 * S * (2 * HEADS + 2 * CT + 2 * KT) + 4 * QT * AW
    q_lo = at("q_lo", [P, S], F32R, swapped_at)
    k_lo = at("k_lo", [P, S], F32R, swapped_at + 4 * S)
    q_scaled = at("q_scaled", [P, S], F32, swapped_at + 8 * S)
    x_tok = at("x_tok", [P, QT, DM], F32, shared)
    squares = at("squares", [P, BT, S], F32, shared + 3 * 4 * DM)
    lambdas = at("lambdas", [P, DEPTH, 2, 2, HD], F32, shared + 4 * QT * DM)
    lam_prod = at("lam_prod", [P, DEPTH * 2, HD], F32, shared + 4 * (QT * DM + DEPTH * 4 * HD))
    lam_sum = at("lam_sum", [P, DEPTH * 2], F32, shared + 4 * (QT * DM + DEPTH * 6 * HD))
    lam_exp = at("lam_exp", [P, DEPTH * 2], F32, shared + 4 * (QT * DM + DEPTH * 6 * HD + 16))
    lam_dif = at("lam_dif", [P, DEPTH], F32, shared + 4 * (QT * DM + DEPTH * 6 * HD + 32))

    bank = [nc.alloc_psum_tensor(f"bank{i}", [P, COLS], F32) for i in range(8)]
    SCORE = [bank[4], bank[5]]
    TURN = bank[6]
    MIX = bank[7]

    sem = nc.alloc_semaphore
    raw_landed = [sem(f"raw_landed{i}") for i in range(NRAW)]
    x_landed = [sem(f"x_landed{i}") for i in range(BT)]
    ident_landed = sem("ident_landed")
    small_landed = sem("small_landed")
    lam_landed = sem("lam_landed")
    tables_landed = sem("tables_landed")
    swap_landed = sem("swap_landed")
    stored = sem("stored")
    stored_2 = sem("stored_2")
    tile_done = sem("tile_done")
    unit_released = sem("unit_released")
    squares_summed = sem("squares_summed")
    rms_spread = sem("rms_spread")
    scores_done = sem("scores_done")
    turned = sem("turned")
    heads_mixed = sem("heads_mixed")
    heads_turned = sem("heads_turned")
    hi_ready = sem("hi_ready")
    low_copied = sem("low_copied")
    xg_hi = sem("xg_hi")
    squared = sem("squared")
    lam_exped = sem("lam_exped")
    silu_done = sem("silu_done")
    hidden_hi = sem("hidden_hi")
    conv_mid = sem("conv_mid")
    conv_hi = sem("conv_hi")
    probs_done = sem("probs_done")
    wt_copied = sem("wt_copied")
    o_squared = sem("o_squared")
    o_hi = sem("o_hi")
    out_ready_2 = sem("out_ready_2")
    weights_ready = sem("weights_ready")
    bank_free = sem("bank_free")
    set_up = sem("set_up")
    lam_step = sem("lam_step")
    x_updated = sem("x_updated")
    xg_ready = sem("xg_ready")
    sq_added = sem("sq_added")
    ms_ready = sem("ms_ready")
    rms_copied = sem("rms_copied")
    tables_ready = sem("tables_ready")
    rope_step = sem("rope_step")
    rope_done = sem("rope_done")
    gate_stored = sem("gate_stored")
    z_ready = sem("z_ready")
    conv_step = sem("conv_step")
    conv_ready = sem("conv_ready")
    max_ready = sem("max_ready")
    w_step = sem("w_step")
    o_scaled = sem("o_scaled")
    o_ready = sem("o_ready")
    gate_scaled = sem("gate_scaled")
    up_scaled = sem("up_scaled")
    hidden_f32 = sem("hidden_f32")
    hidden_ready = sem("hidden_ready")
    out_scaled = sem("out_scaled")
    out_ready = sem("out_ready")
    x_squared = sem("x_squared")
    rms_ready = sem("rms_ready")
    stage_step = sem("stage_step")
    staged = sem("staged")
    o_ms_ready = sem("o_ms_ready")
    o_rms_ready = sem("o_rms_ready")
    gated = sem("gated")

    ds = bass.ds
    lo_bits = lambda ap: ap.bitcast(F32)

    def over_tiles(ap):
        return ap.unsqueeze(1).to_broadcast([P, BT, S])

    w_in_v = w_in.rearrange("l (t p) n -> p l t n", p=P)
    w_out_v = w_out.rearrange("l (t p) n -> p l t n", p=P)
    w_gate_v = w_gate.rearrange("l (t p) n -> p l t n", p=P)
    w_up_v = w_up.rearrange("l (t p) n -> p l t n", p=P)
    w_down_v = w_down.rearrange("l (t p) n -> p l t n", p=P)

    def constants_set(eng):
        eng.wait_ge(set_up, 4)

    with nc.Block() as block:

        @block.sync
        def _(sp):
            x_v = x.rearrange("o (q p) n -> p (o q) n", p=P)
            sp.dma_start(ident[:], ident_d).then_inc(ident_landed, 16)
            for c in range(BT):
                sp.dma_start(x_tok[:, :, COLS * c:COLS * (c + 1)], x_v[:, :, COLS * c:COLS * (c + 1)]
                             ).then_inc(x_landed[c], 16)

            def slot_free(load, prior):
                sp.wait_ge(weights_ready, load * 2 + (SPLIT_BIAS + 2 - 2 * prior))

            def rows(slot, half):
                return raw[:, slot, UNIT_KT * half:UNIT_KT * (half + 1), :].unsqueeze(1)

            def load(src, layer, number, slot, kts, col, prior=NRAW):
                slot_free(number, prior)
                for half in range(2):
                    t = kts[UNIT_KT * half]
                    sp.dma_start(rows(slot, half), src[:, ds(layer, 1), t:t + UNIT_KT, ds(col, COLS)]
                                 ).then_inc(raw_landed[slot], 16)

            def plain_block(src, layer, b, col, order=tuple(range(KT)), priors=(NRAW,) * NRAW):
                for j in range(LOADS):
                    load(src, layer, layer * (UNITS_LAYER // 2) + (b * LOADS + j), j,
                         order[LOAD_KT * j:LOAD_KT * (j + 1)], col, priors[j])

            with sp.Fori(0, DEPTH) as layer:
                plain_block(w_in_v, layer, 0, 0, priors=(2, 2, 4, 4))
                with sp.Fori(1, OUT0) as b:
                    plain_block(w_in_v, layer, b, b * COLS)
                with sp.Fori(OUT0, GU0) as b:
                    plain_block(w_out_v, layer, b, b * COLS - OUT0 * COLS, order=OUT_ORDER)
                with sp.Fori(GU0, DOWN0) as b:
                    for j in range(LOADS):
                        slot_free(layer * (UNITS_LAYER // 2) + (b * LOADS + j), NRAW)
                        for half, src in ((0, w_gate_v), (1, w_up_v)):
                            sp.dma_start(raw[:, j, :, half * S:(half + 1) * S].unsqueeze(1),
                                         src[:, ds(layer, 1), LOAD_KT * j:LOAD_KT * (j + 1),
                                             ds(b * S - GU0 * S, S)]).then_inc(raw_landed[j], 16)
                with sp.Fori(0, NDOWN // 2) as pair:
                    for j in range(2 * DLOADS):
                        k = LOAD_KT * (j % DLOADS)
                        load(w_down_v, layer,
                             layer * (UNITS_LAYER // 2) + (pair * (2 * DLOADS) + DOWN0 * LOADS + j),
                             j % NRAW, range(k, k + LOAD_KT),
                             pair * (2 * COLS) + j // DLOADS * COLS, 2 if j < 2 else NRAW)
            for c in range(BT):
                sp.wait_ge(out_ready, c + 1)
                sp.dma_start(out[0, 0:P, COLS * c:COLS * (c + 1)],
                             x_tok[:, 0, COLS * c:COLS * (c + 1)]).then_inc(stored, 16)
            sp.wait_ge(stored, 16 * BT)

        @block.gpsimd
        def _(pool):
            pool.dma_start(lambdas[:], lambdas_d).then_inc(lam_landed, 16)

            def rms(norm):
                pool.wait_ge(ms_ready, norm + 1)
                pool.tensor_tensor(rms_tok[:], mean_sq[:], neg_half[:], ALU.pow).then_inc(rms_ready, 1)

            def swap(layer, c):
                pool.wait_ge(bank_free, layer * TILES_LAYER + (c * BT + PRE + BT))
                for r in range(4):
                    pool.dma_start(swapped[32 * r:32 * r + 32],
                                   qk[32 * (r ^ 1):32 * (r ^ 1) + 32, ds(c * BT, BT), :]).then_inc(swap_landed, 16)

            def stage(layer, h):
                q, k = qk[:, ds(h, 1), :], qk[:, ds(h + HEADS, 1), :]
                tile = lambda ap: ap[:].unsqueeze(1)
                scale = tile(q_scale).to_broadcast([P, 1, S])
                constants_set(pool)
                pool.tensor_tensor(tile(q_scaled), q, scale, ALU.mult).then_inc(stage_step, 1)
                pool.tensor_tensor(tile(q_hi), q, scale, ALU.mult).then_inc(stage_step, 1)
                pool.tensor_copy(tile(k_hi), k).then_inc(stage_step, 1)
                pool.wait_ge(stage_step, layer * (3 * HEADS) + (h * 3 + 3))
                constants_set(pool)
                pool.tensor_tensor(tile(q_lo), tile(q_scaled), lo_bits(tile(q_hi)), ALU.subtract)
                pool.tensor_tensor(tile(k_lo), k, lo_bits(tile(k_hi)), ALU.subtract).then_inc(staged, 1)

            def head_rms(layer, h):
                pool.wait_ge(o_squared, layer * HEADS + (h + 1))
                pool.tensor_tensor(o_ms[:], o_sq[:], inv_width[:], ALU.mult).then_inc(o_ms_ready, 1)
                pool.wait_ge(o_ms_ready, layer * (2 * HEADS) + (h * 2 + 1))
                pool.tensor_tensor(o_ms[:], o_ms[:], eps[:], ALU.add).then_inc(o_ms_ready, 1)
                pool.wait_ge(o_ms_ready, layer * (2 * HEADS) + (h * 2 + 2))
                pool.tensor_tensor(o_rms[:], o_ms[:], neg_half[:], ALU.pow).then_inc(o_rms_ready, 1)

            def gate(layer, u):
                for j in range(BT):
                    pool.wait_ge(conv_step, layer * (2 * CT) + (2 * BT * u + BT + j + 1))
                    pool.tensor_tensor(ev[:, j, :], ev[:, j, :], gates[:, BT * u + j, :], ALU.mult).then_inc(gated, 1)

            pool.wait_ge(sq_added, EARLY_TILES + 1)
            half = BT // 2
            for c in range(EARLY_TILES // BT):
                tiles = resid[:, BT * c:BT * (c + 1), :]
                pool.wait_ge(bank_free, BT * (c + 1))
                if c > 0:
                    pool.wait_ge(x_squared, 4 * c)
                pool.tensor_tensor(squares[:], tiles, tiles, ALU.mult).then_inc(x_squared, 1)
                pool.wait_ge(x_squared, 4 * c + 1)
                pool.tensor_tensor(squares[:, 0:half, :], squares[:, 0:half, :], squares[:, half:BT, :], ALU.add
                                   ).then_inc(x_squared, 1)
                for i in range(half):
                    pool.wait_ge(x_squared, 4 * c + 2 + i)
                    pool.tensor_tensor(sqacc[:], sqacc[:], squares[:, i, :], ALU.add).then_inc(x_squared, 1)

            with pool.Fori(0, DEPTH) as layer:
                rms(layer * 2)
                with pool.Fori(0, NQK) as c:
                    pool.wait_ge(rope_done, layer * NQK + (c + 1))
                    swap(layer, c)
                pool.wait_ge(rope_done, layer * NQK + (NQK + 1))
                stage(layer, 0)
                pool.wait_ge(scores_done, layer * HEADS + 1)
                stage(layer, 1)
                head_rms(layer, 0)
                with pool.Fori(2, HEADS - 1) as h:
                    pool.wait_ge(scores_done, layer * HEADS + h)
                    stage(layer, h)
                    head_rms(layer, h - 1)
                pool.wait_ge(scores_done, layer * HEADS + (HEADS - 1))
                stage(layer, HEADS - 1)
                gate(layer, 0)
                head_rms(layer, HEADS - 2)
                head_rms(layer, HEADS - 1)
                gate(layer, 1)
                rms(layer * 2 + 1)
            rms(2 * DEPTH)

        @block.scalar
        def _(act):
            def split(blk, first, last):
                for k in range(first, last):
                    if k % 2 == 0:
                        act.wait_ge(raw_landed[blk.raw_slot(k)], blk.landed(k))
                    if k < 2:
                        act.wait_ge(unit_released, blk.released + (k - 1))
                    elif k < NSPLIT:
                        act.wait_ge(tile_done, blk.tile0)
                    else:
                        act.wait_ge(unit_released, blk.released + (k - NSPLIT + 1))
                    act.activation(whi[:, blk.slot(k)], raw[:, blk.raw_slot(k), k % 2 * UNIT_KT:(k % 2 + 1) * UNIT_KT, :],
                                   ACT.Copy).then_inc(hi_ready, 1)

            def low_halves(blk, ev_free=None):
                if ev_free is not None:
                    act.wait_ge(ev_free[0], ev_free[1])
                for j in range(BT):
                    act.wait_ge(tile_done, blk.tile0 + (j + 1))
                    act.activation(ev[:, j, :], bank[j][:, S:2 * S], ACT.Copy).then_inc(low_copied, 1)

            def normed(tile, j, gain):
                constants_set(act)
                act.activation(xg[:, ds(tile, 1), 0:S], resid[:, ds(tile, 1), :], ACT.Copy,
                               scale=consts[:, ds(gain, 1)]).then_inc(xg_hi, 1)
                act.activation(ev[:, j, :].unsqueeze(1), resid[:, ds(tile, 1), :], ACT.Square).then_inc(squared, 1)

            def residual(layer, c, ffn):
                for j in range(BT):
                    act.wait_ge(x_updated, layer * (2 * KT) + (c * BT + (0 if ffn else KT) + BT + j + 1))
                    normed(c * BT + j, j, layer * KT + (c * BT + j + (C_FFN if ffn else C_MIX + KT)))

            def conv(layer, u):
                for j in range(BT):
                    act.wait_ge(z_ready, layer * CT + (BT * u + j + 1))
                    constants_set(act)
                    act.activation(ev[:, j, :], gates[:, CT + BT * u + j, :], ACT.Copy,
                                   scale=consts[:, ds(layer * (3 * CT) + (C_CONV + CT + BT * u + j), 1)]
                                   ).then_inc(conv_mid, 1)

            def conv_out(layer, u):
                for j in range(BT):
                    act.wait_ge(gated, layer * CT + (BT * u + j + 1))
                    act.activation(mixed[:, HEADS + BT * u + j, 0:S], ev[:, j, :], ACT.Copy).then_inc(conv_hi, 1)

            def silu(layer, g):
                for j in range(2):
                    act.wait_ge(gate_scaled, layer * FT + (g * 2 + j + 1))
                    act.activation(ev[:, 2 * j, :], ev[:, 2 * j, :], ACT.Silu).then_inc(silu_done, 1)

            def hidden_out(layer, g):
                for j in range(2):
                    act.wait_ge(hidden_f32, layer * FT + (g * 2 + j + 1))
                    constants_set(act)
                    act.activation(hidden[:, ds(g * 2 + j, 1), 0:S], ev[:, 2 * j + 1, :].unsqueeze(1), ACT.Copy
                                   ).then_inc(hidden_hi, 1)

            def exps(layer, h):
                act.wait_ge(max_ready, layer * (2 * HEADS) + (h * 2 + 2))
                for m in range(2):
                    for q in range(QT):
                        c = m * QT + q
                        last = act.activation(probs[:, m, q, :], SCORE[m][:, S * q:S * (q + 1)], ACT.Exp,
                                              bias=neg_max[:, c:c + 1], accum_out=exp_sum[:, c:c + 1])
                last.then_inc(probs_done, 1)

            def copy_weights(layer, h):
                act.wait_ge(turned, layer * HEADS + (h + 1))
                act.activation(wt[:].rearrange("p k q -> p (k q)"), TURN[:], ACT.Copy).then_inc(wt_copied, 1)

            def head_squares(layer, h):
                act.wait_ge(heads_mixed, layer * HEADS + (h + 1))
                for q in range(QT):
                    last = act.activation(o_tok[:, q, :], MIX[:, P * q:P * (q + 1)], ACT.Square,
                                          accum_out=o_sq[:, q:q + 1])
                last.then_inc(o_squared, 1)

            def head_out(layer, h):
                constants_set(act)
                act.wait_ge(heads_turned, layer * HEADS + (h + 1))
                act.activation(mixed[:, ds(h, 1), 0:S], MIX[:, S:2 * S].unsqueeze(1), ACT.Copy,
                               scale=sub_gain[:, ds(layer, 1)]).then_inc(o_hi, 1)

            def sq_added_at(layer, norm, c):
                return layer * (2 * (KT + 1)) + (c * BT + norm * (KT + 1) + 1)

            act.dma_start(consts[:], consts_d).then_inc(small_landed, 16)
            act.wait_ge(lam_step, 2)
            act.activation(lam_exp[:], lam_sum[:], ACT.Exp).then_inc(lam_exped, 1)
            constants_set(act)
            for t in range(EARLY_TILES):
                act.wait_ge(bank_free, t + 1)
                act.activation(xg[:, t, 0:S], resid[:, t, :], ACT.Copy, scale=consts[:, C_MIX + t:C_MIX + t + 1]
                               ).then_inc(xg_hi, 1)

            with act.Fori(0, DEPTH) as layer:
                blk = Place(layer, 0)
                split(blk, 0, 2)
                low_halves(LastPlace(layer), (sq_added, sq_added_at(layer, 0, BT - 1)))
                act.dma_start(cos_r[:], tables_d[0]).then_inc(tables_landed, 16)
                act.dma_start(sin_r[:], tables_d[1]).then_inc(tables_landed, 16)
                split(blk, 2, 4)
                residual(layer - 1, NOUT - 1, False)
                split(blk, 4, UNITS)
                prev = Place(layer, 0)
                blk = Place(layer, 1)
                split(blk, 0, 2)
                low_halves(prev, (sq_added, sq_added_at(layer, 0, NOUT)))
                split(blk, 2, UNITS)
                with act.Fori(2, NQK) as b:
                    blk = EarlyPlace(layer, b)
                    split(blk, 0, 2)
                    low_halves(EarlyPlace(layer, b - 1))
                    split(blk, 2, UNITS)
                blk = Place(layer, V0)
                split(blk, 0, 2)
                low_halves(Place(layer, V0 - 1))
                split(blk, 2, UNITS)
                blk = Place(layer, V0 + 1)
                split(blk, 0, 6)
                exps(layer, 0)
                split(blk, 6, UNITS)
                copy_weights(layer, 0)
                exps(layer, 1)
                head_squares(layer, 0)

                def conv_block(b, ev_free, finish=None):
                    h = b - V0
                    blk = Place(layer, b)
                    split(blk, 0, 2)
                    if ev_free is False:
                        head_out(layer, 0)
                    copy_weights(layer, h - 1)
                    if ev_free is not False:
                        low_halves(Place(layer, b - 1), ev_free)
                    split(blk, 2, 4)
                    if finish is not None:
                        conv(layer, finish)
                    split(blk, 4, 6)
                    head_squares(layer, h - 1)
                    split(blk, 6, 7)
                    if finish is not None:
                        conv_out(layer, finish)
                    exps(layer, h)
                    head_out(layer, h - 1)
                    split(blk, 7, UNITS)

                conv_block(B0, False)
                conv_block(B0 + 1, None)
                with act.Fori(C0, U0 + 1) as b:
                    conv_block(b, (gate_stored, layer * (2 * CT) + (b * BT - C0 * BT + BT)))
                conv_block(U0 + 1, (gate_stored, layer * (2 * CT) + 2 * CT), finish=0)

                blk = Place(layer, OUT0)
                split(blk, 0, 2)
                copy_weights(layer, HEADS - 1)
                low_halves(Place(layer, OUT0 - 1), (conv_ready, layer * CT + BT))
                split(blk, 2, 4)
                conv(layer, 1)
                split(blk, 4, 6)
                head_squares(layer, HEADS - 1)
                conv_out(layer, 1)
                split(blk, 6, 7)
                head_out(layer, HEADS - 1)
                split(blk, 7, UNITS)
                blk = Place(layer, OUT0 + 1)
                split(blk, 0, 2)
                low_halves(Place(layer, OUT0), (conv_ready, layer * CT + CT))
                split(blk, 2, 4)
                residual(layer, 0, True)
                split(blk, 4, UNITS)
                with act.Fori(2, NOUT + 1) as c:
                    blk = Place(layer, c + OUT0)
                    split(blk, 0, 2)
                    low_halves(Place(layer, c + (OUT0 - 1)), (sq_added, sq_added_at(layer, 1, c - 1)))
                    split(blk, 2, 4)
                    residual(layer, c - 1, True)
                    split(blk, 4, UNITS)
                blk = Place(layer, GU0 + 1)
                split(blk, 0, 2)
                low_halves(Place(layer, GU0), (sq_added, sq_added_at(layer, 1, NOUT)))
                split(blk, 2, 4)
                silu(layer, 0)
                split(blk, 4, 5)
                hidden_out(layer, 0)
                split(blk, 5, UNITS)
                with act.Fori(2, NGU) as g:
                    blk = Place(layer, g + GU0)
                    split(blk, 0, 2)
                    low_halves(Place(layer, g + (GU0 - 1)), (hidden_ready, layer * FT + (g * 2 - 2)))
                    split(blk, 2, 4)
                    silu(layer, g - 1)
                    split(blk, 4, 5)
                    hidden_out(layer, g - 1)
                    split(blk, 5, UNITS)
                for d in range(NDOWN):
                    blk = Place(layer, None, down=d)
                    split(blk, 0, 2)
                    if d == 0:
                        low_halves(Place(layer, DOWN0 - 1), (hidden_ready, layer * FT + (FT - 2)))
                        split(blk, 2, 4)
                        silu(layer, NGU - 1)
                        split(blk, 4, 5)
                        hidden_out(layer, NGU - 1)
                        split(blk, 5, DUNITS)
                    else:
                        ev_free = ((hidden_ready, layer * FT + FT) if d == 1
                                   else (sq_added, sq_added_at(layer, 2, d - 1)))
                        low_halves(Place(layer, None, down=d - 1), ev_free)
                        split(blk, 2, 4)
                        residual(layer, d - 1, False)
                        split(blk, 4, DUNITS)

            low_halves(LastPlace(DEPTH), (sq_added, sq_added_at(DEPTH, 0, BT - 1)))
            for j in range(BT):
                act.wait_ge(x_updated, DEPTH * 2 * KT + j + 1)
                act.activation(ev[:, j, :], resid[:, EARLY_TILES + j, :], ACT.Square).then_inc(squared, 1)
            act.wait_ge(rms_ready, 2 * DEPTH + 1)
            for c in range(BT):
                act.wait_ge(tile_done, PRE + DEPTH * TILES_LAYER + QT * c + 2)
                act.activation(x_tok[:, 1, COLS * c:COLS * (c + 1)], bank[OUT_BANKS[QT * c + 1]][:], ACT.Copy,
                               scale=rms_tok[:, 1:2]).then_inc(out_ready_2, 1)
                act.wait_ge(out_ready_2, c + 1)
                act.dma_start(out[0, P:2 * P, COLS * c:COLS * (c + 1)],
                              x_tok[:, 1, COLS * c:COLS * (c + 1)]).then_inc(stored_2, 16)
            act.wait_ge(stored_2, 16 * BT)

        @block.vector
        def _(dve):
            def split(blk, first, last):
                for k in range(first, last):
                    dve.wait_ge(hi_ready, blk.unit0 + (k + 1))
                    dve.tensor_tensor(wlo[:, blk.slot(k)], raw[:, blk.raw_slot(k), k % 2 * UNIT_KT:(k % 2 + 1) * UNIT_KT, :],
                                      lo_bits(whi[:, blk.slot(k)]), ALU.subtract).then_inc(weights_ready, 1)

            def sums(blk, qk_block=None):
                for j in range(BT):
                    dve.wait_ge(low_copied, blk.low0 + (j + 1))
                    if qk_block is None:
                        dst = ev[:, j, :]
                        dve.tensor_tensor(dst, bank[j][:, 0:S], ev[:, j, :], ALU.add).then_inc(bank_free, 1)
                    else:
                        dst = qk[:, ds(qk_block * BT + j, 1), :]
                        dve.tensor_tensor(dst, bank[j][:, 0:S].unsqueeze(1), ev[:, j, :].unsqueeze(1), ALU.add
                                          ).then_inc(bank_free, 1)

            def rotate(layer, c):
                tiles = qk[:, ds(c * BT, BT), :]
                dve.wait_ge(tables_ready, layer * 3 + 3)
                dve.wait_ge(swap_landed, layer * (64 * NQK) + (c * 64 + 64))
                dve.tensor_tensor(swapped[:], swapped[:], over_tiles(sin_r[:]), ALU.mult).then_inc(rope_step, 1)
                dve.tensor_tensor(tiles, tiles, over_tiles(cos_r[:]), ALU.mult).then_inc(rope_step, 1)
                dve.wait_ge(rope_step, layer * (2 * NQK) + (c * 2 + 2))
                dve.tensor_tensor(tiles, tiles, swapped[:], ALU.add).then_inc(rope_done, 1)

            def norm_sums(norm):
                dve.wait_ge(squares_summed, norm + 1)
                dve.tensor_scalar(mean_sq[:], MIX[:, 0:QT], 1.0 / DM, EPS, ALU.mult, ALU.add).then_inc(ms_ready, 1)
                dve.memset(sqacc[:], 0.0).then_inc(sq_added, 1)

            def norm_spread(norm):
                dve.wait_ge(rms_spread, norm + 1)
                dve.tensor_copy(rms_bc[:], MIX[:, S:2 * S]).then_inc(rms_copied, 1)

            def v_out(layer, i):
                blk = Place(layer, V0 + i)
                dve.wait_ge(rms_ready, layer * 2 + 1)
                for q in range(QT):
                    dve.wait_ge(tile_done, blk.tile0 + (q + 1))
                    dve.tensor_scalar(v_tok[:, q, COLS * i:COLS * (i + 1)], bank[QT * i + q][:], rms_tok[:, q:q + 1],
                                      None, ALU.mult).then_inc(bank_free, 1)

            def gate_out(layer, g, scale):
                for j in range(BT):
                    dve.wait_ge(bank_free, layer * TILES_LAYER
                                + (g * BT + PRE + BT * B0 - NV * (BT - QT) + j + 1))
                    dve.tensor_tensor(gates[:, ds(g * BT + j, 1), :], ev[:, j, :].unsqueeze(1), scale[:].unsqueeze(1),
                                      ALU.mult).then_inc(gate_stored, 1)

            def conv_products(layer, u):
                dve.wait_ge(gate_stored, layer * (2 * CT) + 2 * CT)
                for j in range(BT):
                    t = CT + BT * u + j
                    dve.wait_ge(bank_free, Place(layer, U0 + u).tile0 + (j + 1))
                    dve.tensor_tensor(gates[:, t, :], ev[:, j, :], gates[:, t, :], ALU.mult).then_inc(z_ready, 1)

            def conv_neighbours(layer, u):
                for side in range(2):
                    for j in range(BT):
                        t = CT + BT * u + j
                        tap = consts[:, ds(layer * (3 * CT) + (C_CONV + 2 * side * CT + BT * u + j), 1)]
                        step = layer * (2 * CT) + (2 * BT * u + j)
                        if side == 0:
                            dve.wait_ge(conv_mid, layer * CT + (BT * u + j + 1))
                            to, frm = ev[:, j, 1:S], gates[:, t, 0:S - 1]
                        else:
                            dve.wait_ge(conv_step, step + 1)
                            to, frm = ev[:, j, 0:S - 1], gates[:, t, 1:S]
                        dve.scalar_tensor_tensor(to, frm, tap, to, ALU.mult, ALU.add).then_inc(conv_step, 1)

            def conv_low(layer, u):
                for j in range(BT):
                    dve.wait_ge(conv_hi, layer * CT + (BT * u + j + 1))
                    t = HEADS + BT * u + j
                    dve.tensor_tensor(mixed[:, t, S:2 * S], ev[:, j, :], lo_bits(mixed[:, t, 0:S]), ALU.subtract
                                      ).then_inc(conv_ready, 1)

            def row_max(layer, h):
                dve.wait_ge(scores_done, layer * HEADS + (h + 1))
                for m in range(2):
                    dve.reduce_max(neg_max[:, QT * m:QT * (m + 1)], SCORE[m][:].rearrange("p (q k) -> p q k", q=QT),
                                   AX_X, negate=True).then_inc(max_ready, 1)

            def combine(layer, h):
                step = layer * (6 * HEADS) + h * 6
                dve.wait_ge(probs_done, layer * HEADS + (h + 1))
                dve.reciprocal(exp_inv[:], exp_sum[:]).then_inc(w_step, 1)
                dve.wait_ge(w_step, step + 1)
                dve.tensor_scalar(exp_inv[:, QT:2 * QT], exp_inv[:, QT:2 * QT], neg_lam[:, ds(layer, 1)], None,
                                  ALU.mult).then_inc(w_step, 1)
                for q in range(QT):
                    dve.tensor_scalar(probs[:, 0, q, :], probs[:, 0, q, :], exp_inv[:, q:q + 1], None,
                                      ALU.mult).then_inc(w_step, 1)
                for q in range(QT):
                    dve.wait_ge(w_step, step + (3 + q))
                    dve.scalar_tensor_tensor(probs[:, 0, q, :], probs[:, 1, q, :], exp_inv[:, QT + q:QT + q + 1],
                                             probs[:, 0, q, :], ALU.mult, ALU.add).then_inc(w_step, 1)

            def head_scale(layer, h):
                dve.wait_ge(o_rms_ready, layer * HEADS + (h + 1))
                for q in range(QT):
                    dve.tensor_scalar(o_tok[:, q, :], MIX[:, P * q:P * (q + 1)], o_rms[:, q:q + 1], None,
                                      ALU.mult).then_inc(o_scaled, 1)

            def head_low(layer, h):
                dve.wait_ge(o_hi, layer * HEADS + (h + 1))
                dve.scalar_tensor_tensor(mixed[:, ds(h, 1), S:2 * S], MIX[:, S:2 * S].unsqueeze(1),
                                         sub_gain[:, ds(layer, 1)], lo_bits(mixed[:, ds(h, 1), 0:S]),
                                         ALU.mult, ALU.subtract).then_inc(o_ready, 1)

            def add_residual(layer, c, blk):
                for j in range(BT):
                    dve.wait_ge(bank_free, blk.tile0 + (j + 1))
                    t = resid[:, ds(c * BT + j, 1), :]
                    dve.tensor_tensor(t, t, ev[:, j, :].unsqueeze(1), ALU.add).then_inc(x_updated, 1)

            def low_part(norm, tile, gain):
                dve.wait_ge(xg_hi, norm * KT + (tile + 1))
                dve.scalar_tensor_tensor(xg[:, ds(tile, 1), S:2 * S], resid[:, ds(tile, 1), :], consts[:, ds(gain, 1)],
                                         lo_bits(xg[:, ds(tile, 1), 0:S]), ALU.mult, ALU.subtract
                                         ).then_inc(xg_ready, 1)

            def add_square(norm, tile, j):
                dve.wait_ge(squared, norm * KT + (tile + 1 - EARLY_TILES))
                dve.wait_ge(sq_added, norm * (KT + 1) + (tile + 1))
                dve.tensor_tensor(sqacc[:], sqacc[:], ev[:, j, :], ALU.add).then_inc(sq_added, 1)

            def residual_low(layer, c, ffn):
                norm = layer * 2 + (1 if ffn else 2)
                dve.wait_ge(x_squared, SQ_STEPS)
                for j in range(BT):
                    low_part(norm, c * BT + j, layer * KT + (c * BT + j + (C_FFN if ffn else C_MIX + KT)))
                    add_square(norm, c * BT + j, j)

            def scale_gu(layer, g, blk):
                dve.wait_ge(rms_copied, layer * 2 + 2)
                for j in range(2):
                    for tile, done in ((2 * j, gate_scaled), (2 * j + 1, up_scaled)):
                        dve.wait_ge(bank_free, blk.tile0 + (tile + 1))
                        dve.tensor_tensor(ev[:, tile, :], ev[:, tile, :], rms_bc[:], ALU.mult).then_inc(done, 1)

            def hidden_products(layer, g):
                for j in range(2):
                    n = layer * FT + (g * 2 + j + 1)
                    dve.wait_ge(silu_done, n)
                    dve.wait_ge(up_scaled, n)
                    dve.tensor_tensor(ev[:, 2 * j + 1, :], ev[:, 2 * j + 1, :], ev[:, 2 * j, :], ALU.mult
                                      ).then_inc(hidden_f32, 1)

            def hidden_low(layer, g):
                for j in range(2):
                    dve.wait_ge(hidden_hi, layer * FT + (g * 2 + j + 1))
                    t = ds(g * 2 + j, 1)
                    dve.tensor_tensor(hidden[:, t, S:2 * S], ev[:, 2 * j + 1, :].unsqueeze(1),
                                      lo_bits(hidden[:, t, 0:S]), ALU.subtract).then_inc(hidden_ready, 1)

            def copy_x(first):
                for t in range(first, first + BT):
                    dve.wait_ge(tile_done, t + 1)
                    dve.tensor_copy(resid[:, t, :], bank[x_bank(t)][:, 0:S]).then_inc(bank_free, 1)

            dve.memset(ones[:], 1.0).then_inc(weights_ready, SPLIT_BIAS)
            dve.memset(neg_half[:], -0.5).then_inc(set_up, 1)
            dve.memset(q_scale[:], HD ** -0.5).then_inc(set_up, 1)
            dve.memset(inv_width[:], 1.0 / (2 * HD)).then_inc(set_up, 1)
            dve.memset(eps[:], EPS).then_inc(rope_done, 1)
            dve.memset(resid[:, EARLY_TILES:KT, :], 0.0)
            dve.memset(sqacc[:], 0.0).then_inc(sq_added, EARLY_TILES + 1)
            dve.wait_ge(lam_landed, 16)
            dve.tensor_tensor(lam_prod[:].rearrange("p (l m) d -> p l m d", l=DEPTH), lambdas[:, :, :, 0, :],
                              lambdas[:, :, :, 1, :], ALU.mult).then_inc(lam_step, 1)
            dve.wait_ge(lam_step, 1)
            dve.reduce_sum(lam_sum[:], lam_prod[:], AX_X).then_inc(lam_step, 1)
            copy_x(0)
            dve.wait_ge(small_landed, 16)
            for l in range(DEPTH):
                lam_init = 0.8 - 0.6 * math.exp(-0.3 * l)
                dve.tensor_scalar(sub_gain[:, l:l + 1], consts[:, C_SUB + l:C_SUB + l + 1], 1.0 - lam_init, None,
                                  ALU.mult)
            dve.wait_ge(lam_exped, 1)
            for l in range(DEPTH):
                dve.tensor_tensor(lam_dif[:, l:l + 1], lam_exp[:, 2 * l + 1:2 * l + 2], lam_exp[:, 2 * l:2 * l + 1],
                                  ALU.subtract).then_inc(lam_step, 1)
            for l in range(DEPTH):
                lam_init = 0.8 - 0.6 * math.exp(-0.3 * l)
                dve.wait_ge(lam_step, 3 + l)
                last = dve.tensor_scalar(neg_lam[:, l:l + 1], lam_dif[:, l:l + 1], lam_init, None, ALU.subtract)
            last.then_inc(set_up, 1)
            copy_x(BT)
            for t in range(BT):
                low_part(0, t, C_MIX + t)
            copy_x(2 * BT)
            for t in range(BT, EARLY_TILES):
                low_part(0, t, C_MIX + t)

            with dve.Fori(0, DEPTH) as layer:
                blk = Place(layer, 0)
                prev = LastPlace(layer)
                split(blk, 0, 2)
                sums(prev)
                split(blk, 2, 3)
                add_residual(layer, NOUT - 1, prev)
                split(blk, 3, 4)
                residual_low(layer - 1, NOUT - 1, False)
                split(blk, 4, 7)
                norm_sums(layer * 2)
                split(blk, 7, UNITS)
                norm_spread(layer * 2)
                dve.wait_ge(tables_landed, layer * 32 + 32)
                dve.wait_ge(rms_copied, layer * 2 + 1)
                dve.tensor_tensor(cos_r[:], cos_r[:], rms_bc[:], ALU.mult).then_inc(tables_ready, 1)
                dve.tensor_tensor(sin_r[:], sin_r[:], rms_bc[:], ALU.mult).then_inc(tables_ready, 1)
                dve.tensor_tensor(rms2_bc[:], rms_bc[:], rms_bc[:], ALU.mult).then_inc(tables_ready, 1)
                with dve.Fori(1, NQK) as b:
                    blk = EarlyPlace(layer, b)
                    split(blk, 0, 2)
                    sums(EarlyPlace(layer, b - 1), b - 1)
                    split(blk, 2, 6)
                    rotate(layer, b - 1)
                    split(blk, 6, UNITS)
                blk = Place(layer, V0)
                split(blk, 0, 2)
                sums(Place(layer, V0 - 1), NQK - 1)
                split(blk, 2, 7)
                rotate(layer, NQK - 1)
                split(blk, 7, UNITS)
                blk = Place(layer, V0 + 1)
                split(blk, 0, 2)
                v_out(layer, 0)
                split(blk, 2, 6)
                row_max(layer, 0)
                combine(layer, 0)
                split(blk, 6, UNITS)
                row_max(layer, 1)
                combine(layer, 1)
                head_scale(layer, 0)

                def attention_part(blk, h):
                    split(blk, 4, 6)
                    head_scale(layer, h - 1)
                    row_max(layer, h)
                    split(blk, 6, 7)
                    combine(layer, h)
                    split(blk, 7, UNITS)
                    head_low(layer, h - 1)

                blk = Place(layer, B0)
                split(blk, 0, 2)
                head_low(layer, 0)
                v_out(layer, 1)
                split(blk, 2, 4)
                attention_part(blk, 2)
                for kind, scale in ((0, rms_bc), (1, rms2_bc)):
                    with dve.Fori(kind * NG, (kind + 1) * NG) as g:
                        blk = Place(layer, g + (B0 + 1))
                        split(blk, 0, 2)
                        sums(Place(layer, g + B0))
                        split(blk, 2, 3)
                        gate_out(layer, g, scale)
                        split(blk, 3, 4)
                        attention_part(blk, g + 3)
                blk = Place(layer, U0 + 1)
                split(blk, 0, 2)
                sums(Place(layer, U0))
                split(blk, 2, 3)
                conv_products(layer, 0)
                split(blk, 3, 4)
                conv_neighbours(layer, 0)
                split(blk, 4, 6)
                head_scale(layer, HEADS - 2)
                row_max(layer, HEADS - 1)
                split(blk, 6, 7)
                conv_low(layer, 0)
                combine(layer, HEADS - 1)
                split(blk, 7, UNITS)
                head_low(layer, HEADS - 2)
                blk = Place(layer, OUT0)
                split(blk, 0, 2)
                sums(Place(layer, U0 + 1))
                split(blk, 2, 3)
                conv_products(layer, 1)
                split(blk, 3, 4)
                conv_neighbours(layer, 1)
                split(blk, 4, 5)
                head_scale(layer, HEADS - 1)
                split(blk, 5, 6)
                conv_low(layer, 1)
                split(blk, 6, 7)
                head_low(layer, HEADS - 1)
                split(blk, 7, UNITS)
                with dve.Fori(1, NOUT) as c:
                    blk = Place(layer, c + OUT0)
                    prev = Place(layer, c + (OUT0 - 1))
                    split(blk, 0, 2)
                    sums(prev)
                    split(blk, 2, 3)
                    add_residual(layer, c - 1, prev)
                    split(blk, 3, 4)
                    residual_low(layer, c - 1, True)
                    split(blk, 4, UNITS)
                blk = Place(layer, GU0)
                prev = Place(layer, GU0 - 1)
                split(blk, 0, 2)
                sums(prev)
                split(blk, 2, 3)
                add_residual(layer, NOUT - 1, prev)
                split(blk, 3, 4)
                residual_low(layer, NOUT - 1, True)
                split(blk, 4, 7)
                norm_sums(layer * 2 + 1)
                split(blk, 7, UNITS)
                norm_spread(layer * 2 + 1)
                with dve.Fori(1, NGU) as g:
                    blk = Place(layer, g + GU0)
                    prev = Place(layer, g + (GU0 - 1))
                    split(blk, 0, 2)
                    sums(prev)
                    split(blk, 2, 3)
                    scale_gu(layer, g - 1, prev)
                    split(blk, 3, 4)
                    hidden_products(layer, g - 1)
                    split(blk, 4, 5)
                    hidden_low(layer, g - 1)
                    split(blk, 5, UNITS)
                for d in range(NDOWN):
                    blk = Place(layer, None, down=d)
                    split(blk, 0, 2)
                    if d == 0:
                        prev = Place(layer, DOWN0 - 1)
                        sums(prev)
                        split(blk, 2, 3)
                        scale_gu(layer, NGU - 1, prev)
                        split(blk, 3, 4)
                        hidden_products(layer, NGU - 1)
                        split(blk, 4, 5)
                        hidden_low(layer, NGU - 1)
                        split(blk, 5, DUNITS)
                    else:
                        prev = Place(layer, None, down=d - 1)
                        sums(prev)
                        split(blk, 2, 3)
                        add_residual(layer, d - 1, prev)
                        split(blk, 3, 4)
                        residual_low(layer, d - 1, False)
                        split(blk, 4, DUNITS)

            dve.wait_ge(x_updated, DEPTH * 2 * KT)
            for t in range(EARLY_TILES):
                dve.tensor_scalar(resid[:, t, :], resid[:, t, :], consts[:, C_FIN + t:C_FIN + t + 1], None,
                                  ALU.mult).then_inc(out_scaled, 1)
            prev = LastPlace(DEPTH)
            sums(prev)
            add_residual(DEPTH, NOUT - 1, prev)
            for t in range(EARLY_TILES, KT):
                dve.wait_ge(squared, 2 * DEPTH * KT + t + 1 - EARLY_TILES)
                dve.tensor_scalar(resid[:, t, :], resid[:, t, :], consts[:, C_FIN + t:C_FIN + t + 1], None,
                                  ALU.mult).then_inc(out_scaled, 1)
            norm_sums(2 * DEPTH)
            dve.wait_ge(rms_ready, 2 * DEPTH + 1)
            for c in range(BT):
                dve.wait_ge(tile_done, PRE + DEPTH * TILES_LAYER + QT * c + 1)
                dve.tensor_scalar(x_tok[:, 0, COLS * c:COLS * (c + 1)], bank[OUT_BANKS[QT * c]][:], rms_tok[:, 0:1], None,
                                  ALU.mult).then_inc(out_ready, 1)

        @block.tensor
        def _(pe):
            def unit_there(blk, k):
                pe.wait_ge(weights_ready, blk.unit0 + (SPLIT_BIAS + k + 1))

            def products(blk, ks, moving, kts=range(FT), cols=PLAIN):
                for k in ks:
                    unit_there(blk, k)
                for j in range(BT):
                    if ks[0] == 0:
                        pe.wait_ge(bank_free, blk.tile0 + (j + 1 - BT))
                    for k in ks:
                        for i in range(UNIT_KT):
                            kt = kts[UNIT_KT * k + i]
                            w = slice(P * cols[j], P * (cols[j] + 1))
                            pe.matmul(bank[j][:], whi[:, blk.slot(k), i, w], moving[:, kt, :],
                                      start=(k == 0 and i == 0), stop=False, skip_group_check=True)
                            last = pe.matmul(bank[j][:, 0:S], wlo[:, blk.slot(k), i, w], moving[:, kt, 0:S],
                                             start=False, stop=(k == blk.units - 1 and i == UNIT_KT - 1),
                                             skip_group_check=True)
                        if j == BT - 1 and k < blk.units - 2:
                            last.then_inc(unit_released, 1)
                    if ks[-1] == blk.units - 1:
                        last.then_inc(tile_done, 1)

            def v_products(blk, i, ks):
                for k in ks:
                    unit_there(blk, k)
                for q in range(QT):
                    b = bank[QT * i + q]
                    if ks[0] == 0:
                        pe.wait_ge(bank_free, blk.tile0 + (q + 1 - BT))
                    for k in ks:
                        for r in range(UNIT_KT):
                            kt = UNIT_KT * k + r
                            x_hi = xg[:, kt, P * q:P * (q + 1)]
                            x_lo = xg[:, kt, S + P * q:S + P * (q + 1)]
                            w_hi, w_lo = whi[:, blk.slot(k), r, :], wlo[:, blk.slot(k), r, :]
                            final = k == blk.units - 1 and r == UNIT_KT - 1
                            pe.matmul(b[:], x_hi, w_hi, start=(k == 0 and r == 0), stop=False)
                            pe.matmul(b[:], x_hi, w_lo, start=False, stop=False)
                            last = pe.matmul(b[:], x_lo, w_hi, start=False, stop=final)
                        if q == QT - 1 and k < blk.units - 2:
                            last.then_inc(unit_released, 1)
                    if ks[-1] == blk.units - 1:
                        last.then_inc(tile_done, 1)

            def sum_squares(norm, tiles=()):
                pe.wait_ge(sq_added, norm * (KT + 1) + (KT + 1 - len(tiles)))
                if tiles:
                    pe.wait_ge(squared, norm * KT + (KT - EARLY_TILES))
                parts = [sqacc[:]] + [ev[:, j, :] for j in tiles]
                for q in range(QT):
                    for i, part in enumerate(parts):
                        last = pe.matmul(MIX[:, q:q + 1], part[:, P * q:P * (q + 1)], ones[:], start=(i == 0),
                                         stop=(i == len(parts) - 1))
                last.then_inc(squares_summed, 1)

            def spread_rms(norm):
                pe.wait_ge(rms_ready, norm + 1)
                for q in range(QT):
                    last = pe.matmul(MIX[:, S + P * q:S + P * (q + 1)], rms_tok[:, q:q + 1].to_broadcast([P, P]), ident[:],
                                     start=True, stop=True)
                last.then_inc(rms_spread, 1)

            def scores(layer, h):
                pe.wait_ge(staged, layer * HEADS + (h + 1))
                if not isinstance(h, int) or h > 0:
                    pe.wait_ge(probs_done, layer * HEADS + h)
                parts = ((q_hi, k_hi), (q_hi, k_lo), (q_lo, k_hi))
                for q in range(QT):
                    for i, (q_part, k_part) in enumerate(parts):
                        for m in range(2):
                            rows = slice(HD * m, HD * (m + 1))
                            last = pe.matmul(SCORE[m][:, S * q:S * (q + 1)], q_part[rows, P * q:P * (q + 1)],
                                             k_part[rows, :], start=(i == 0), stop=(i == len(parts) - 1))
                last.then_inc(scores_done, 1)

            def turn_weights(layer, h):
                pe.wait_ge(w_step, layer * (6 * HEADS) + (h * 6 + 6))
                for k in range(QT):
                    for q in range(QT):
                        last = pe.transpose(TURN[:, S * k + P * q:S * k + P * (q + 1)],
                                            probs[:, 0, q, P * k:P * (k + 1)], ident[:])
                last.then_inc(turned, 1)

            def mix(layer, h):
                pe.wait_ge(wt_copied, layer * HEADS + (h + 1))
                if isinstance(h, int) and h == 0:
                    pe.wait_ge(rms_copied, layer * 2 + 1)
                else:
                    pe.wait_ge(o_ready, layer * HEADS + h)
                for q in range(QT):
                    for k in range(QT):
                        last = pe.matmul(MIX[:, P * q:P * (q + 1)].unsqueeze(1), wt[:, k, P * q:P * (q + 1)],
                                         v_tok[:, k:k + 1, ds(h * P, P)], start=(k == 0), stop=(k == QT - 1))
                last.then_inc(heads_mixed, 1)

            def turn_head(layer, h):
                pe.wait_ge(o_scaled, layer * (QT * HEADS) + (h * QT + QT))
                for q in range(QT):
                    last = pe.transpose(MIX[:, S + P * q:S + P * (q + 1)], o_tok[:, q, :], ident[:])
                last.then_inc(heads_turned, 1)

            def first_block(blk, norm, cols):
                def tiles_ready(k):
                    pe.wait_ge(xg_ready, norm * KT + (UNIT_KT * k + UNIT_KT))

                tiles_ready(1)
                products(blk, [0, 1], xg, cols=cols)
                for k in range(2, UNITS - 2):
                    tiles_ready(k)
                    products(blk, [k], xg, cols=cols)
                    if k == 3:
                        sum_squares(norm)
                    if k == 5:
                        spread_rms(norm)
                tiles_ready(UNITS - 1)
                products(blk, [UNITS - 2, UNITS - 1], xg, cols=cols)

            pe.wait_ge(ident_landed, 16)
            for t in range(KT):
                pe.wait_ge(x_landed[t // BT], 16)
                if t >= 2 * BT:
                    pe.wait_ge(bank_free, t - 2 * BT + 1)
                for q in range(QT):
                    last = pe.transpose(bank[x_bank(t)][:, P * q:P * (q + 1)], x_tok[:, q, P * t:P * (t + 1)], ident[:])
                    if t == 0 and q == 0:
                        last.then_inc(unit_released, RELEASE_BIAS)
                if t >= EARLY_TILES:
                    pe.wait_ge(sq_added, EARLY_TILES + 1)
                    for q in range(QT):
                        last = pe.transpose(bank[x_bank(t)][:, S + P * q:S + P * (q + 1)], resid[:, t, P * q:P * (q + 1)],
                                            ident[:])
                last.then_inc(tile_done, 1)

            with pe.Fori(0, DEPTH) as layer:
                first_block(Place(layer, 0), layer * 2, PLAIN)
                with pe.Fori(1, NQK) as b:
                    blk = EarlyPlace(layer, b)
                    products(blk, [0, 1], xg)
                    for k in range(2, UNITS - 2):
                        products(blk, [k], xg)
                    products(blk, [UNITS - 2, UNITS - 1], xg)
                blk = Place(layer, V0)
                v_products(blk, 0, [0, 1])
                for k in range(2, UNITS - 2):
                    v_products(blk, 0, [k])
                v_products(blk, 0, [UNITS - 2, UNITS - 1])
                blk = Place(layer, V0 + 1)
                v_products(blk, 1, [0, 1])
                scores(layer, 0)
                v_products(blk, 1, [2])
                v_products(blk, 1, [3])
                v_products(blk, 1, [4])
                turn_weights(layer, 0)
                scores(layer, 1)
                v_products(blk, 1, [5])
                pe.wait_ge(bank_free, blk.tile0)
                mix(layer, 0)
                v_products(blk, 1, [UNITS - 2, UNITS - 1])
                turn_head(layer, 0)
                turn_weights(layer, 1)
                with pe.Fori(B0, OUT0) as b:
                    h = b - V0
                    blk = Place(layer, b)
                    products(blk, [0, 1], xg)
                    mix(layer, h - 1)
                    products(blk, [2], xg)
                    scores(layer, h)
                    products(blk, [3], xg)
                    turn_head(layer, h - 1)
                    products(blk, [4], xg)
                    products(blk, [5], xg)
                    turn_weights(layer, h)
                    products(blk, [6, 7], xg)
                blk = Place(layer, OUT0)
                pe.wait_ge(o_ready, layer * HEADS + (HEADS - 2))
                products(blk, [0, 1], mixed, OUT_ORDER)
                mix(layer, HEADS - 1)
                products(blk, [2], mixed, OUT_ORDER)
                pe.wait_ge(conv_ready, layer * CT + BT)
                products(blk, [3], mixed, OUT_ORDER)
                turn_head(layer, HEADS - 1)
                products(blk, [4], mixed, OUT_ORDER)
                pe.wait_ge(conv_ready, layer * CT + CT)
                products(blk, [5], mixed, OUT_ORDER)
                pe.wait_ge(o_ready, layer * HEADS + HEADS)
                products(blk, [6, 7], mixed, OUT_ORDER)
                with pe.Fori(1, NOUT) as c:
                    blk = Place(layer, c + OUT0)
                    products(blk, [0, 1], mixed, OUT_ORDER)
                    for k in range(2, UNITS - 2):
                        products(blk, [k], mixed, OUT_ORDER)
                    products(blk, [UNITS - 2, UNITS - 1], mixed, OUT_ORDER)
                first_block(Place(layer, GU0), layer * 2 + 1, GU_COLS)
                with pe.Fori(1, NGU) as g:
                    blk = Place(layer, g + GU0)
                    products(blk, [0, 1], xg, cols=GU_COLS)
                    for k in range(2, UNITS - 2):
                        products(blk, [k], xg, cols=GU_COLS)
                    products(blk, [UNITS - 2, UNITS - 1], xg, cols=GU_COLS)
                with pe.Fori(0, NDOWN // 2) as pair:
                    pe.wait_ge(hidden_ready, layer * FT + (FT - 2))
                    for half in range(2):
                        blk = Place(layer, None, down=half)
                        n = pair * 2
                        blk.unit0 = blk.unit0 + n * DUNITS
                        blk.tile0 = blk.tile0 + n * BT
                        products(blk, [0, 1], hidden)
                        for k in range(2, DUNITS - 2):
                            products(blk, [k], hidden)
                        if half == 0:
                            pe.wait_ge(hidden_ready, layer * FT + FT)
                        products(blk, [DUNITS - 2, DUNITS - 1], hidden)

            for g in range(QT * BT):
                c, q = divmod(g, QT)
                b = OUT_BANKS[g]
                pe.wait_ge(out_scaled, BT * (c + 1))
                if b < BT:
                    pe.wait_ge(bank_free, PRE + DEPTH * TILES_LAYER - BT + b + 1)
                elif g >= BT:
                    pe.wait_ge(out_ready, 1)
                for i in range(BT):
                    last = pe.transpose(bank[b][:, P * i:P * (i + 1)], resid[:, BT * c + i, P * q:P * (q + 1)], ident[:])
                last.then_inc(tile_done, 1)
                if g == BT - 1:
                    sum_squares(2 * DEPTH, PLAIN)


def kernel(x, norm_mix, w_in, lambda_q1, lambda_k1, lambda_q2, lambda_k2, subln, conv_w, w_out, norm_ffn,
           w_gate, w_up, w_down, norm_final):
    import concourse.bacc as bacc
    from concourse.bass_utils import run_bass_kernel_spmd

    arr = np.ascontiguousarray

    def tiled(v):
        v = np.asarray(v)
        return v.reshape(-1, P).T

    consts = arr(np.concatenate([tiled(norm_mix), tiled(norm_final), tiled(norm_ffn), tiled(conv_w), tiled(subln)],
                                axis=1))
    lam = np.stack([np.stack([np.asarray(lambda_q1), np.asarray(lambda_k1)], 1),
                    np.stack([np.asarray(lambda_q2), np.asarray(lambda_k2)], 1)], 1)
    lam = arr(np.broadcast_to(lam[None], (P,) + lam.shape))
    half = HD // 2
    inv = np.float32(THETA) ** (-np.arange(0, HD, 2, dtype=np.float32) / np.float32(HD))
    ang = np.arange(S, dtype=np.float32)[None, :] * inv[np.arange(P) % half][:, None]
    sign = np.where(np.arange(P) % HD < half, np.float32(-1), np.float32(1))[:, None]
    tables = arr(np.stack([np.cos(ang), np.sin(ang) * sign]).astype(np.float32))

    nc = bacc.Bacc("TRN2", target_bir_lowering=False, num_devices=1)
    ins = {"x": arr(x), "w_in": arr(w_in), "w_out": arr(w_out), "w_gate": arr(w_gate), "w_up": arr(w_up),
           "w_down": arr(w_down), "consts": consts, "lambdas": lam, "tables": tables,
           "ident": np.eye(P, dtype=np.float32)}
    args = [nc.dram_tensor(f"{n}_dram", a.shape, mybir.dt.from_np(a.dtype), kind="ExternalInput").ap()
            for n, a in ins.items()]
    out = nc.dram_tensor("out_dram", (1, S, DM), F32, kind="ExternalOutput").ap()
    build_program(nc, *args, out)
    r = run_bass_kernel_spmd(nc, [{f"{n}_dram": a for n, a in ins.items()}], core_ids=[0])
    return r.results[0]["out_dram"]
```
